# Optimizing a Trainium2 kernel written in Bass

```python
import jax, jax.numpy as jnp
from jax import lax
import numpy as np
import math

D_MODEL = 1024
BATCH = 1
SEQ = 512
DEPTH = 2

N_MIXERS = 2
N_RET_LAYERS = (DEPTH + 1) // 2
N_MLA_LAYERS = DEPTH // 2

ROPE_BASE = 10000.0
NORM_EPS = 1e-6

RET_HEADS = 4
RET_QK_DIM = D_MODEL // RET_HEADS
RET_V_DIM = 2 * RET_QK_DIM
RET_WIDTH = RET_HEADS * RET_V_DIM
RET_CHUNK = 128

MLA_HEADS = 16
MLA_NOPE = 128
MLA_ROPE = 64
MLA_V = 128
Q_LORA = 3 * D_MODEL // 4
KV_LORA = D_MODEL // 4
MLA_WIDTH = MLA_HEADS * MLA_V
Q_BLOCK = 128

PLE_DIM = 256


def rms_norm(x, g):
    xf = x.astype(jnp.float32)
    y = xf * lax.rsqrt(jnp.mean(xf * xf, axis=-1, keepdims=True) + NORM_EPS)
    return (y * g.astype(jnp.float32)).astype(x.dtype)

def rope(x, pos):
    half = x.shape[-1] // 2
    inv_freq = ROPE_BASE ** (-jnp.arange(half, dtype=jnp.float32) / half)
    ang = pos.astype(jnp.float32)[..., None] * inv_freq
    cos = jnp.cos(ang)[:, :, None, :]
    sin = jnp.sin(ang)[:, :, None, :]
    xf = x.astype(jnp.float32)
    x1, x2 = xf[..., :half], xf[..., half:]
    return jnp.concatenate([x1 * cos - x2 * sin, x2 * cos + x1 * sin], axis=-1).astype(x.dtype)

def retention_branch(h, pos, w_in, gn_g, w_out):
    B, S, _ = h.shape
    n_chunks = S // RET_CHUNK
    z = h @ w_in
    qk_w = RET_HEADS * RET_QK_DIM
    q = z[..., :qk_w].reshape(B, S, RET_HEADS, RET_QK_DIM)
    k = z[..., qk_w:2 * qk_w].reshape(B, S, RET_HEADS, RET_QK_DIM)
    v = z[..., 2 * qk_w:2 * qk_w + RET_WIDTH].reshape(B, S, RET_HEADS, RET_V_DIM)
    gate = z[..., 2 * qk_w + RET_WIDTH:]
    q = rope(q, pos)
    k = rope(k, pos) * (RET_QK_DIM ** -0.5)

    log_g = jnp.log(1.0 - 2.0 ** (-5.0 - jnp.arange(RET_HEADS, dtype=jnp.float32)))
    idx = jnp.arange(RET_CHUNK, dtype=jnp.float32)
    rel = idx[:, None] - idx[None, :]
    dmask = jnp.where(rel[None] >= 0, jnp.exp(jnp.maximum(rel, 0.0)[None] * log_g[:, None, None]), 0.0)
    q_decay = jnp.exp((idx + 1.0)[None, :] * log_g[:, None])
    k_decay = jnp.exp((RET_CHUNK - 1.0 - idx)[None, :] * log_g[:, None])
    c_decay = jnp.exp(RET_CHUNK * log_g)

    def to_chunks(t):
        return t.astype(jnp.float32).reshape(B, n_chunks, RET_CHUNK, RET_HEADS, t.shape[-1]).transpose(1, 0, 3, 2, 4)

    qc, kc, vc = to_chunks(q), to_chunks(k), to_chunks(v)

    def step(state, inp):
        qb, kb, vb = inp
        a = jnp.einsum('bhid,bhjd->bhij', qb, kb) * dmask
        o = jnp.einsum('bhij,bhjv->bhiv', a, vb) + jnp.einsum(
            'bhid,bhdv->bhiv', qb * q_decay[..., None], state)
        state = state * c_decay[:, None, None] + jnp.einsum(
            'bhjd,bhjv->bhdv', kb * k_decay[..., None], vb)
        return state, o

    s0 = jnp.zeros((B, RET_HEADS, RET_QK_DIM, RET_V_DIM), jnp.float32)
    _, o = lax.scan(step, s0, (qc, kc, vc))
    o = o.transpose(1, 0, 3, 2, 4).reshape(B, S, RET_HEADS, RET_V_DIM)
    o = o * lax.rsqrt(jnp.mean(o * o, axis=-1, keepdims=True) + NORM_EPS)
    o = (o.reshape(B, S, RET_WIDTH) * gn_g.astype(jnp.float32)).astype(h.dtype)
    return (jax.nn.silu(gate) * o) @ w_out

def mla_branch(h, pos, w_in, q_norm_g, kv_norm_g, w_uq, w_uk, w_uv, w_out):
    B, S, _ = h.shape
    n_blocks = S // Q_BLOCK
    z = h @ w_in
    o1, o2, o3 = Q_LORA, Q_LORA + KV_LORA, Q_LORA + KV_LORA + MLA_ROPE
    c_q = rms_norm(z[..., :o1], q_norm_g)
    c_kv = rms_norm(z[..., o1:o2], kv_norm_g)
    k_rope = rope(z[..., o2:o3][:, :, None, :], pos)[:, :, 0, :]
    gate = z[..., o3:]

    q = (c_q @ w_uq).reshape(B, S, MLA_HEADS, MLA_NOPE + MLA_ROPE)
    q_nope = q[..., :MLA_NOPE]
    q_rope = rope(q[..., MLA_NOPE:], pos)
    q_abs = jnp.einsum('bshd,chd->bshc', q_nope, w_uk)
    scale = (MLA_NOPE + MLA_ROPE) ** -0.5
    q_cat = jnp.concatenate([q_abs, q_rope], axis=-1) * scale
    k_cat = jnp.concatenate([c_kv, k_rope], axis=-1)
    q_blocks = q_cat.reshape(B, n_blocks, Q_BLOCK, MLA_HEADS, -1).transpose(1, 0, 2, 3, 4)
    key_idx = jnp.arange(S)
    neg = jnp.finfo(jnp.float32).min

    def attend(args):
        qb, bi = args
        s = jnp.einsum('bqhc,bkc->bhqk', qb, k_cat).astype(jnp.float32)
        q_idx = bi * Q_BLOCK + jnp.arange(Q_BLOCK)
        s = jnp.where(key_idx[None, :] <= q_idx[:, None], s, neg)
        pr = jax.nn.softmax(s, axis=-1).astype(c_kv.dtype)
        return jnp.einsum('bhqk,bkc->bqhc', pr, c_kv)

    o_lat = lax.map(attend, (q_blocks, jnp.arange(n_blocks)))
    o_lat = o_lat.transpose(1, 0, 2, 3, 4).reshape(B, S, MLA_HEADS, KV_LORA)
    o = jnp.einsum('bshc,chd->bshd', o_lat, w_uv).reshape(B, S, MLA_WIDTH)
    return (jax.nn.silu(gate) * o) @ w_out

def first_inputs(seed: int = 0) -> dict:
    key = jax.random.key(seed)
    ks = jax.random.split(key, 20)
    f32 = jnp.float32

    def w(k, shape, fan_in):
        return jax.random.normal(k, shape, f32) * (fan_in ** -0.5)

    def gain(k, shape):
        return 1.0 + 0.02 * jax.random.normal(k, shape, f32)

    ret_in_w = 2 * RET_HEADS * RET_QK_DIM + 2 * RET_WIDTH
    mla_in_w = Q_LORA + KV_LORA + MLA_ROPE + MLA_WIDTH
    offset = jax.random.randint(ks[2], (BATCH, 1), 0, 4096, dtype=jnp.int32)
    return {
        "x": jax.random.normal(ks[0], (BATCH, SEQ, D_MODEL), f32),
        "p": jax.random.normal(ks[1], (DEPTH, BATCH, SEQ, PLE_DIM), f32),
        "positions": offset + jnp.arange(SEQ, dtype=jnp.int32)[None, :],
        "pre_norm_g": gain(ks[3], (DEPTH, D_MODEL)),
        "post_norm_g": gain(ks[4], (DEPTH, D_MODEL)),
        "ret_w_in": w(ks[5], (N_RET_LAYERS, D_MODEL, ret_in_w), D_MODEL),
        "ret_gn_g": gain(ks[6], (N_RET_LAYERS, RET_WIDTH)),
        "ret_w_out": w(ks[7], (N_RET_LAYERS, RET_WIDTH, D_MODEL), RET_WIDTH),
        "mla_w_in": w(ks[8], (N_MLA_LAYERS, D_MODEL, mla_in_w), D_MODEL),
        "mla_q_norm_g": gain(ks[9], (N_MLA_LAYERS, Q_LORA)),
        "mla_kv_norm_g": gain(ks[10], (N_MLA_LAYERS, KV_LORA)),
        "mla_w_uq": w(ks[11], (N_MLA_LAYERS, Q_LORA, MLA_HEADS * (MLA_NOPE + MLA_ROPE)), Q_LORA),
        "mla_w_uk": w(ks[12], (N_MLA_LAYERS, KV_LORA, MLA_HEADS, MLA_NOPE), KV_LORA),
        "mla_w_uv": w(ks[13], (N_MLA_LAYERS, KV_LORA, MLA_HEADS, MLA_V), KV_LORA),
        "mla_w_out": w(ks[14], (N_MLA_LAYERS, MLA_WIDTH, D_MODEL), MLA_WIDTH),
        "ple_w_proj": w(ks[15], (DEPTH, PLE_DIM, D_MODEL), PLE_DIM),
        "ple_w_gate": w(ks[16], (DEPTH, D_MODEL, D_MODEL), D_MODEL),
    }

def first_block(x, p, positions, pre_norm_g, post_norm_g, ret_w_in, ret_gn_g, ret_w_out,
              mla_w_in, mla_q_norm_g, mla_kv_norm_g, mla_w_uq, mla_w_uk, mla_w_uv, mla_w_out,
              ple_w_proj, ple_w_gate):
    for i in range(DEPTH):
        h = rms_norm(x, pre_norm_g[i])
        j = i // N_MIXERS
        if i % N_MIXERS == 0:
            y = retention_branch(h, positions, ret_w_in[j], ret_gn_g[j], ret_w_out[j])
        else:
            y = mla_branch(h, positions, mla_w_in[j], mla_q_norm_g[j], mla_kv_norm_g[j],
                           mla_w_uq[j], mla_w_uk[j], mla_w_uv[j], mla_w_out[j])
        x = x + rms_norm(y, post_norm_g[i])
        x = x + (p[i] @ ple_w_proj[i]) * jax.nn.sigmoid(x @ ple_w_gate[i])
    return x


N_A_LAYERS = (DEPTH + 1) // 2
N_B_LAYERS = DEPTH // 2

CHUNK = 128
GATE_WIDTH = D_MODEL
GATE_GROUPS = 8
GATE_GROUP_DIM = GATE_WIDTH // GATE_GROUPS

WINDOW_DILATIONS = ((128, 1), (512, 4), (2048, 16))
N_DIL_GROUPS = len(WINDOW_DILATIONS)
ATT_HEADS = 8
HEAD_DIM = 64
ATT_WIDTH = ATT_HEADS * HEAD_DIM

N_BUCKETS = 32
MAX_EXACT = N_BUCKETS // 2
REL_MAX_DISTANCE = max(w for w, _ in WINDOW_DILATIONS)

D_FF = 4 * D_MODEL

EPS = 1e-6
NEG_INF = -1e30


def _rms_norm(x, g):
    xf = x.astype(jnp.float32)
    y = xf * lax.rsqrt(jnp.mean(xf * xf, axis=-1, keepdims=True) + EPS)
    return (y * g.astype(jnp.float32)).astype(x.dtype)

def _layer_norm(x, g, b):
    xf = x.astype(jnp.float32)
    mu = jnp.mean(xf, axis=-1, keepdims=True)
    xc = xf - mu
    y = xc * lax.rsqrt(jnp.mean(xc * xc, axis=-1, keepdims=True) + EPS)
    return (y * g.astype(jnp.float32) + b.astype(jnp.float32)).astype(x.dtype)

def _t5_bucket(distance):
    small = distance < MAX_EXACT
    nf = jnp.maximum(distance, 1).astype(jnp.float32)
    large = MAX_EXACT + (jnp.log(nf / MAX_EXACT) / math.log(REL_MAX_DISTANCE / MAX_EXACT)
                         * (N_BUCKETS - MAX_EXACT)).astype(jnp.int32)
    large = jnp.minimum(large, N_BUCKETS - 1)
    return jnp.where(small, distance, large)

def _chunk_gating_mixer(h, w_in, ln_g, ln_b, w_s, b_s, w_out):
    B_, S_, _ = h.shape
    uv = jax.nn.gelu(h @ w_in, approximate=False)
    u, v = jnp.split(uv, 2, axis=-1)
    v = _layer_norm(v, ln_g, ln_b)
    nc = S_ // CHUNK
    v = v.reshape(B_, nc, CHUNK, GATE_GROUPS, GATE_GROUP_DIM)
    causal = jnp.tril(jnp.ones((CHUNK, CHUNK), dtype=bool))
    w = jnp.where(causal[None], w_s, 0.0)
    mixed = jnp.einsum('gts,bnsgc->bntgc', w, v) + b_s.T[None, None, :, :, None]
    gate = mixed.reshape(B_, S_, GATE_WIDTH)
    return (u * gate) @ w_out

def _dilated_group(q, k, v, bias_table, window, dilation):
    B_, S_, H, hd = q.shape
    blk = window // dilation
    span = blk * dilation
    Sp = -(-S_ // span) * span
    nb = Sp // span

    def split(t):
        t = jnp.pad(t, ((0, 0), (0, Sp - S_), (0, 0), (0, 0)))
        return t.reshape(B_, nb, blk, dilation, H, hd)

    def with_prev(t):
        prev = jnp.pad(t, ((0, 0), (1, 0), (0, 0), (0, 0), (0, 0), (0, 0)))[:, :-1]
        return jnp.concatenate([prev, t], axis=2)

    qb = split(q)
    kc = with_prev(split(k))
    vc = with_prev(split(v))

    s = jnp.einsum('bnqrhc,bnkrhc->bnrhqk', qb, kc) * (HEAD_DIM ** -0.5)
    rel = blk + jnp.arange(blk)[:, None] - jnp.arange(2 * blk)[None, :]
    band = (rel >= 0) & (rel <= blk)
    bucket = _t5_bucket(jnp.clip(rel, 0, blk) * dilation)
    bias = jnp.transpose(bias_table[bucket], (2, 0, 1))
    first = (jnp.arange(nb)[:, None, None] == 0) & (jnp.arange(2 * blk)[None, None, :] < blk)
    valid = band[None] & ~first
    logits = jnp.where(valid[None, :, None, None], s + bias[None, None, None], NEG_INF)

    m = jnp.max(logits, axis=-1)
    p = jnp.exp(logits - m[..., None])
    den = jnp.sum(p, axis=-1)
    num = jnp.einsum('bnrhqk,bnkrhc->bnqrhc', p, vc)

    num = num.reshape(B_, Sp, H, hd)[:, :S_]
    den = jnp.transpose(den, (0, 1, 4, 2, 3)).reshape(B_, Sp, H)[:, :S_]
    m = jnp.transpose(m, (0, 1, 4, 2, 3)).reshape(B_, Sp, H)[:, :S_]
    return num, den, m

def _dilated_attention_mixer(h, w_qkv, w_out, rel_bias):
    B_, S_, _ = h.shape
    qkv = (h @ w_qkv).astype(jnp.float32).reshape(B_, S_, 3, N_DIL_GROUPS, ATT_HEADS, HEAD_DIM)
    rb = rel_bias.astype(jnp.float32)
    nums, dens, maxs = [], [], []
    for g, (window, dil) in enumerate(WINDOW_DILATIONS):
        n_, d_, m_ = _dilated_group(qkv[:, :, 0, g], qkv[:, :, 1, g], qkv[:, :, 2, g],
                                    rb[:, g * ATT_HEADS:(g + 1) * ATT_HEADS], window, dil)
        nums.append(n_)
        dens.append(d_)
        maxs.append(m_)
    m_all = jnp.max(jnp.stack(maxs), axis=0)
    scales = [jnp.exp(m_ - m_all) for m_ in maxs]
    num_sum = sum(n_ * c[..., None] for n_, c in zip(nums, scales))
    den_sum = sum(d_ * c for d_, c in zip(dens, scales))
    o = (num_sum / den_sum[..., None]).astype(h.dtype).reshape(B_, S_, ATT_WIDTH)
    return o @ w_out

def second_inputs(seed: int = 0) -> dict:
    key = jax.random.key(seed)
    ks = jax.random.split(key, 16)
    f32 = jnp.float32
    nrm = lambda k, shape, s: jax.random.normal(k, shape, f32) * s
    qkv_cols = 3 * N_DIL_GROUPS * ATT_HEADS * HEAD_DIM
    return {
        "x": jax.random.normal(ks[0], (BATCH, SEQ, D_MODEL), f32),
        "mix_norm_g": 1.0 + nrm(ks[1], (DEPTH, D_MODEL), 0.05),
        "mlp_norm_g": 1.0 + nrm(ks[2], (DEPTH, D_MODEL), 0.05),
        "final_norm_g": 1.0 + nrm(ks[3], (D_MODEL,), 0.05),
        "a_w_in": nrm(ks[4], (N_A_LAYERS, D_MODEL, 2 * GATE_WIDTH), D_MODEL ** -0.5),
        "a_ln_g": 1.0 + nrm(ks[5], (N_A_LAYERS, GATE_WIDTH), 0.05),
        "a_ln_b": nrm(ks[6], (N_A_LAYERS, GATE_WIDTH), 0.02),
        "a_w_s": nrm(ks[7], (N_A_LAYERS, GATE_GROUPS, CHUNK, CHUNK), CHUNK ** -0.5),
        "a_b_s": 1.0 + nrm(ks[8], (N_A_LAYERS, GATE_GROUPS, CHUNK), 0.1),
        "a_w_out": nrm(ks[9], (N_A_LAYERS, GATE_WIDTH, D_MODEL), GATE_WIDTH ** -0.5),
        "b_w_qkv": nrm(ks[10], (N_B_LAYERS, D_MODEL, qkv_cols), D_MODEL ** -0.5),
        "b_w_out": nrm(ks[11], (N_B_LAYERS, ATT_WIDTH, D_MODEL), ATT_WIDTH ** -0.5),
        "rel_bias": nrm(ks[12], (N_BUCKETS, N_DIL_GROUPS * ATT_HEADS), 0.5),
        "w_up": nrm(ks[13], (DEPTH, D_MODEL, D_FF), D_MODEL ** -0.5),
        "w_down": nrm(ks[14], (DEPTH, D_FF, D_MODEL), D_FF ** -0.5),
    }

def second_block(x, mix_norm_g, mlp_norm_g, final_norm_g, a_w_in, a_ln_g, a_ln_b, a_w_s, a_b_s,
              a_w_out, b_w_qkv, b_w_out, rel_bias, w_up, w_down):
    h = x
    for layer in range(DEPTH):
        y = _rms_norm(h, mix_norm_g[layer])
        j = layer // N_MIXERS
        if layer % N_MIXERS == 0:
            y = _chunk_gating_mixer(y, a_w_in[j], a_ln_g[j], a_ln_b[j], a_w_s[j], a_b_s[j], a_w_out[j])
        else:
            y = _dilated_attention_mixer(y, b_w_qkv[j], b_w_out[j], rel_bias)
        h = h + y
        y = _rms_norm(h, mlp_norm_g[layer])
        h = h + jnp.square(jax.nn.relu(y @ w_up[layer])) @ w_down[layer]
    return _rms_norm(h, final_norm_g)


def setup_inputs(seed=0):
    out = dict(first_inputs(seed))
    for name, value in second_inputs(seed + 1).items():
        if name != "x":
            out[name + "_2"] = value
    return out


def reference(
    x, p, positions, pre_norm_g, post_norm_g, ret_w_in, ret_gn_g, ret_w_out, mla_w_in,
    mla_q_norm_g, mla_kv_norm_g, mla_w_uq, mla_w_uk, mla_w_uv, mla_w_out, ple_w_proj,
    ple_w_gate, mix_norm_g_2, mlp_norm_g_2, final_norm_g_2, a_w_in_2, a_ln_g_2, a_ln_b_2,
    a_w_s_2, a_b_s_2, a_w_out_2, b_w_qkv_2, b_w_out_2, rel_bias_2, w_up_2, w_down_2,
):
    x = first_block(
        x, p, positions, pre_norm_g, post_norm_g, ret_w_in, ret_gn_g, ret_w_out, mla_w_in,
        mla_q_norm_g, mla_kv_norm_g, mla_w_uq, mla_w_uk, mla_w_uv, mla_w_out, ple_w_proj,
        ple_w_gate,
    )
    return second_block(
        x, mix_norm_g_2, mlp_norm_g_2, final_norm_g_2, a_w_in_2, a_ln_g_2, a_ln_b_2, a_w_s_2,
        a_b_s_2, a_w_out_2, b_w_qkv_2, b_w_out_2, rel_bias_2, w_up_2, w_down_2,
    )


_drawn_inputs = setup_inputs


def setup_inputs(seed=0):
    import zlib

    import numpy as np

    out = dict(_drawn_inputs(seed))
    spreads = {}
    factors = {'ret_gn_g': 2.903,
     'mla_q_norm_g': 5.091,
     'mla_kv_norm_g': 3.189,
     'a_ln_g_2': 4.807,
     'a_ln_b_2': 8.0}
    for name, (base, spread) in spreads.items():
        noise = np.random.default_rng([zlib.crc32(name.encode()), seed]).standard_normal(out[name].shape)
        drawn = base * np.exp(spread * noise) if base else spread * noise
        out[name] = __import__('jax').numpy.asarray(drawn.astype(out[name].dtype))
    for name, factor in factors.items():
        out[name] = (out[name] * factor).astype(out[name].dtype)
    return out
```

```python
from contextlib import ExitStack

import numpy as np

import concourse.bass as bass
from concourse import mybir

D_MODEL, SEQ = 1024, 512
KD = D_MODEL // 128
NT = SEQ // 128
RET_HEADS, RET_QK, RET_V = 4, 256, 512
MLA_HEADS, NOPE, ROPE, MLA_V = 16, 128, 64, 128
Q_LORA, KV_LORA = 768, 256
KQ, KC = Q_LORA // 128, KV_LORA // 128
PAIRS = MLA_HEADS // 2
GROUPS = 8
D_FF = 4096
HID = 512
CHUNKS = D_FF // HID
DILATIONS = (1, 4, 16)
HEAD_DIM = 64
EPS = 1e-6
NEG = -1e30
PANEL = 2048

N_RET = 0
N_PLE0 = N_RET + 8 * RET_HEADS
N_MLAIN = N_PLE0 + 5
N_MLA = N_MLAIN + 5
N_PLE1 = N_MLA + 4 * PAIRS
N_MIX = N_PLE1 + 5
N_MLP0 = N_MIX + 12
N_DIL = N_MLP0 + 4 * CHUNKS
N_DILOUT = N_DIL + 18
N_MLP1 = N_DILOUT + 2
NPANEL = N_MLP1 + 4 * CHUNKS

GAINS = (("pre0", 8), ("post0", 8), ("pre1", 8), ("post1", 8), ("mix0", 8), ("mlp0", 8), ("mix1", 8),
         ("mlp1", 8), ("final", 8), ("qn", KQ), ("kvn", KC), ("lng", GROUPS), ("lnb", GROUPS))
GAIN_AT, _at = {}, 0
for _name, _n in GAINS:
    GAIN_AT[_name] = _at
    _at += _n
NGAIN = _at

def _parts(value, bits, n):
    out, rest = [], value
    for _ in range(n):
        e = np.floor(np.log2(rest))
        q = 2.0 ** (e - bits + 1)
        part = np.floor(rest / q) * q
        out.append(float(part))
        rest -= part
    return out


TWO_PI = 2.0 * np.pi
COARSE = 2.0 ** 15


class Signals(dict):

    def __init__(self, make):
        super().__init__()
        self.make = make

    def __missing__(self, name):
        self[name] = self.make(name)
        return self[name]


NORMS = ("pre0", "post0", "pre1", "cq", "ckv", "post1", "mix0", "mlp0", "mix1", "mlp1", "final")
FULL = tuple(n for n in NORMS if n not in ("cq", "ckv"))
SPLIT = ("pre0", "pre1", "mix0", "mlp0", "mix1", "mlp1")


class BankUses:
    GIVEN = (0, 1, 2, 3, 7)

    def __init__(self):
        self.n = [int(b in self.GIVEN) for b in range(8)]
        self.i, self.per = None, None

    def loop(self, i, per):
        self.i, self.per, self.start = i, per, list(self.n)

    def end(self, trips):
        assert [a - b for a, b in zip(self.n, self.start)] == list(self.per), (self.n, self.start)
        self.n = [s + trips * p for s, p in zip(self.start, self.per)]
        self.i = None

    def take(self, b):
        v = self.n[b]
        self.n[b] += 1
        if self.i is None:
            return v
        return v + self.i * self.per[b]


def program(nc, panels, gains, xin, pin, pos, gn, decay, consts, rel, onehot, wsT, bs, out, scratch, xsave):
    f32, f32r = mybir.dt.float32, mybir.dt.float32r
    ALU, ACT, AX = mybir.AluOpType, mybir.ActivationFunctionType, mybir.AxisListType
    i32 = mybir.dt.int32
    MLA_SCALE = float(NOPE + ROPE) ** -0.5
    ctx = ExitStack()
    with ctx:
        def sb(name, shape, dt=f32, c=ctx):
            return c.enter_context(nc.sbuf_tensor(name, shape, dt))

        S = Signals(lambda name: ctx.enter_context(nc.semaphore(name)))
        B = [ctx.enter_context(nc.psum_tensor(f"bank{b}", [128, 512], f32)) for b in range(8)]
        free = [S[f"bank{b}_free"] for b in range(8)]

        RAW = sb("RAW", [128, 2, PANEL])
        WH = sb("WH", [128, 2, PANEL], f32r)
        WL = sb("WL", [128, 2, PANEL], f32r)
        HH = sb("HH", [128, KD, 512], f32r)
        HL = sb("HL", [128, KD, 512], f32r)
        ACC = sb("ACC", [128, KD, 512])
        G = sb("G", [128, NGAIN])
        CONST = sb("CONST", [128, 3 * 128 + 8])
        IDENT, CAUSAL, UPPER = (CONST[:, 128 * j:128 * j + 128] for j in range(3))
        FREQ1, FREQ2, SIGN = (CONST[:, 384 + j:385 + j] for j in range(3))
        ONES = sb("ONES", [128, 128])
        EPSC = sb("EPSC", [128, 2])
        R = sb("R", [128, 512])
        SS = sb("SS", [128, 512])
        SQ = sb("SQ", [128, 2, 512])
        T = sb("T", [128, 4, 512])
        TG = sb("TG", [128, 2, 512])
        ST = sb("ST", [128, 8, 4])

        with ExitStack() as c:
            CQH, CQL = sb("CQH", [128, KQ, 512], f32r, c), sb("CQL", [128, KQ, 512], f32r, c)
            CKH, CKL = sb("CKH", [128, KC, 512], f32r, c), sb("CKL", [128, KC, 512], f32r, c)
            KRH, KRL = sb("KRH", [128, 512], f32r, c), sb("KRL", [128, 512], f32r, c)
            MQH, MQL = sb("MQH", [128, 4, 512], f32r, c), sb("MQL", [128, 4, 512], f32r, c)
            QRH, QRL = sb("QRH", [128, 512], f32r, c), sb("QRL", [128, 512], f32r, c)
            MVH, MVL = sb("MVH", [128, NT, 256], f32r, c), sb("MVL", [128, NT, 256], f32r, c)
            PKH, PKL = sb("PKH", [128, 1280], f32r, c), sb("PKL", [128, 1280], f32r, c)
            COS2, SIN2 = sb("COS2", [128, 512], f32, c), sb("SIN2", [128, 512], f32, c)
            MU = sb("MU", [128, 2, 512], f32, c)
        MYH, MYL = MQH, MQL
        X = sb("X", [128, KD, 512])
        with ExitStack() as c:
            QH, QL = sb("QH", [128, 2, 512], f32r, c), sb("QL", [128, 2, 512], f32r, c)
            KH, KL = sb("KH", [128, 2, 512], f32r, c), sb("KL", [128, 2, 512], f32r, c)
            VH, VL = sb("VH", [128, NT, 512], f32r, c), sb("VL", [128, NT, 512], f32r, c)
            AH, AL = sb("AH", [128, 4, 512], f32r, c), sb("AL", [128, 4, 512], f32r, c)
            YH, YL = AH, AL
            U = sb("U", [128, 4, 512], f32, c)
            O = sb("O", [128, 4, 512], f32, c)
            COS1, SIN1 = sb("COS1", [128, 512], f32, c), sb("SIN1", [128, 512], f32, c)
            DEC = sb("DEC", [128, 512], f32, c)
            GN = sb("GN", [128, 4], f32, c)
        with ExitStack() as c:
            PJ = sb("PJ", [128, KD, 512], f32, c)
            PF = sb("PF", [128, 2, 512], f32, c)
            PH, PL = sb("PH", [128, 2, 512], f32r, c), sb("PL", [128, 2, 512], f32r, c)
        with ExitStack() as c:
            HIDH, HIDL = sb("HIDH", [128, 4, 512], f32r, c), sb("HIDL", [128, 4, 512], f32r, c)
        with ExitStack() as c:
            NVH, NVL = sb("NVH", [128, NT, 1024], f32r, c), sb("NVL", [128, NT, 1024], f32r, c)
            WTH, WTL = sb("WTH", [128, GROUPS, 128], f32r, c), sb("WTL", [128, GROUPS, 128], f32r, c)
            WT = sb("WT", [128, GROUPS, 128], f32, c)
            BT = sb("BT", [128, GROUPS, 128], f32, c)
            BS = sb("BS", [128, GROUPS, 128], f32, c)
            GU = sb("GU", [128, GROUPS, 512], f32, c)
        NV = ACC[:, :, :].rearrange("p k n -> p (k n)").rearrange("p (t n) -> p t n", t=NT)
        with ExitStack() as c:
            DQH, DQL = sb("DQH", [128, 2, 512], f32r, c), sb("DQL", [128, 2, 512], f32r, c)
            DKH, DKL = sb("DKH", [128, 2, 512], f32r, c), sb("DKL", [128, 2, 512], f32r, c)
            DVH, DVL = sb("DVH", [128, NT, 256], f32r, c), sb("DVL", [128, NT, 256], f32r, c)
            DPH, DPL = sb("DPH", [128, 2, 512], f32r, c), sb("DPL", [128, 2, 512], f32r, c)
            DYH, DYL = sb("DYH", [128, 4, 512], f32r, c), sb("DYL", [128, 4, 512], f32r, c)
            TAB = sb("TAB", [128, 4, 8, 128], f32, c)
            OG1 = sb("OG1", [128, 3, 512], f32, c)
            MXS = sb("MXS", [128, 3, 4, 4], f32, c)
            SUMS = sb("SUMS", [128, 3, 4, 4], f32, c)
        OG = [ACC[:, 0:3, :], OG1[:, :, :]]
        LSE_COLS = [TG[:, 0, :], TG[:, 1, :], T[:, 2, :]]
        LSE, TOP, DY = ACC[:, 3:6, :], T[:, 3, :], SQ[:, 0, :]
        REL = ST[0:33, :, :].rearrange("p a b -> p (a b)")[:, 0:24]
        ONEHOT = TG[0:33, :, :]
        ROWS = ACC[0:24, 0:2, :]
        ROWS8 = [ACC[8 * g:8 * g + 8, 0:2, :] for g in range(3)]

        def in_order(t, g):
            return t[:, :].rearrange("p (r a) -> p r a", r=4)

        def natural(t, g):
            return t[:, :].rearrange("p (r a) -> p r a", r=4) if g == 0 else t[:, :].rearrange("p (a r) -> p r a", r=4)

        def tile_done(e, sig, f, per, n, before=0, base=0):
            if f % per == per - 1:
                e.wait_ge(panel_used, n + 1)
            else:
                e.wait_ge(S[sig], before + (base + (f // per) * (per - 1) + f % per + 1))

        raw_loaded = (S["raw_even_loaded"], S["raw_odd_loaded"])
        hi_ready, lo_ready, panel_used = S["panel_hi_ready"], S["panel_lo_ready"], S["panel_used"]

        block = ctx.enter_context(nc.Block())

        @block.sync
        def _(sp):
            def load(m, slot):
                sp.dma_start(RAW[:, slot, :], panels[m]).then_inc(raw_loaded[slot], 16)

            load(0, 0)
            load(1, 1)
            with sp.Fori(0, (NPANEL - 3) // 2) as i:
                for s in (0, 1):
                    m = sp.snap(i * 2 + (2 + s))
                    sp.wait_ge(lo_ready, i * 2 + (1 + s))
                    sp.dma_start(RAW[:, s, :], panels[bass.ds(m, 1)].rearrange("a p c -> (a p) c"))\
                      .then_inc(raw_loaded[s], 16)
            sp.wait_ge(lo_ready, NPANEL - 2)
            load(NPANEL - 1, (NPANEL - 1) % 2)
            for k in range(KD):
                sp.wait_ge(S["final_ready"], k + 1)
                sp.dma_start(out[k], ACC[:, k, :]).then_inc(S["out_stored"], 16)
            sp.wait_ge(S["out_stored"], 16 * KD)

        @block.gpsimd
        def _(gp):
            def low(s):
                return gp.tensor_tensor(WL[:, s, :], RAW[:, s, :], WH[:, s, :].bitcast(f32), ALU.subtract)

            for m in (0, 1):
                gp.wait_ge(hi_ready, m + 1)
                low(m).then_inc(lo_ready, 1)
            with gp.Fori(0, (NPANEL - 3) // 2) as i:
                for s in (0, 1):
                    gp.wait_ge(hi_ready, i * 2 + (3 + s))
                    gp.wait_ge(panel_used, i * 2 + (1 + s))
                    low(s).then_inc(lo_ready, 1)
            gp.wait_ge(hi_ready, NPANEL)
            gp.wait_ge(panel_used, NPANEL - 2)
            low((NPANEL - 1) % 2).then_inc(lo_ready, 1)

        @block.tensor
        def _(pe):
            uses = BankUses()

            def bank(b):
                v = uses.take(b)
                if not isinstance(v, int) or v > 0:
                    pe.wait_ge(free[b], v)
                return B[b]

            def panel(n, slot):
                pe.wait_ge(lo_ready, n + 1)
                return WH[:, slot, :], WL[:, slot, :]

            def signal(end, sig, last):
                end.then_inc(panel_used if last else S[sig], 1)

            def mm3(o, ah, al, bh, bl, start, stop):
                nc.tensor.matmul(o, ah, bh, start=start, stop=False)
                nc.tensor.matmul(o, ah, bl, start=False, stop=False)
                return nc.tensor.matmul(o, al, bh, start=False, stop=stop)

            def tile_of(o, w, f, width, xh, xl, k0, k1, first=True, last=True, at=0, wait=None):
                wh, wl = w
                for k in range(k0, k1):
                    if wait is not None:
                        wait(k)
                    c = at + (k - k0) * width + f * 128
                    end = mm3(o, wh[:, c:c + 128], wl[:, c:c + 128], xh[:, k, :], xl[:, k, :],
                              first and k == k0, last and k == k1 - 1)
                return end

            def sum_of_squares(name, squares=SS[:, :]):
                o = bank(4)
                pe.wait_ge(S["norm_squares"], NORMS.index(name) + 1)
                nc.tensor.matmul(o[:, :], ONES[:, :], squares, start=True, stop=True).then_inc(S["norm_sum"], 1)

            def of_h(name):
                return lambda k: pe.wait_ge(S["norm_h_split"], KD * SPLIT.index(name) + k + 1)

            pe.wait_ge(S["rel_loaded"], 32)
            pe.wait_ge(S["rel_neg"], 1)
            for j in (0, 1):
                nc.tensor.matmul(bank(5 + j)[0:24, :], REL, ONEHOT[:, j, :], start=True, stop=True)\
                  .then_inc(S["bias_rows"], 1)
            sum_of_squares("pre0")

            with pe.Fori(0, RET_HEADS) as h:
                uses.loop(h, [5] * 4 + [3, 2, 2, 2])
                n = h * 8
                wait_h = of_h("pre0")
                for j in range(2):
                    w = panel(n + j, j % 2)
                    for f in range(2):
                        o = bank(2 * j + f)
                        end = tile_of(o[:, :], w, f, 256, HH, HL, 0, KD, wait=wait_h if j + f == 0 else None)
                    end.then_inc(panel_used, 1)
                os_ = [bank(tt) for tt in range(NT)]
                for j in range(2):
                    wh, wl = panel(n + 2 + j, j % 2)
                    for tt in range(NT):
                        ts = slice(128 * tt, 128 * tt + 128)
                        for k in range(4):
                            end = mm3(os_[tt][:, :], HH[:, 4 * j + k, ts], HL[:, 4 * j + k, ts],
                                      wh[:, 512 * k:512 * k + 512], wl[:, 512 * k:512 * k + 512],
                                      j == 0 and k == 0, j == 1 and k == 3)
                        if j == 1 or tt == NT - 1:
                            signal(end, "ret_v_made", tt == NT - 1)
                pe.wait_ge(S["ret_qk_split"], h * 4 + 4)
                for jt in range(NT):
                    o = bank(4 + jt)
                    for dk in range(2):
                        ks, qs = slice(128 * jt, 128 * jt + 128), slice(128 * jt, 512)
                        end = mm3(o[:, 0:512 - 128 * jt], KH[:, dk, ks], KL[:, dk, ks], QH[:, dk, qs], QL[:, dk, qs],
                                  dk == 0, dk == 1)
                    end.then_inc(S["ret_a_made"], 1)
                w = panel(n + 4, 0)
                for f in range(2):
                    end = tile_of(bank(f)[:, :], w, f, 256, HH, HL, 0, KD)
                    signal(end, "ret_g_made", f == 1)
                pe.wait_ge(S["ret_v_split"], h * 4 + 4)
                for vt in range(4):
                    o = bank(4 + vt)
                    vs = slice(128 * vt, 128 * vt + 128)
                    for jt in range(NT):
                        if vt == 0:
                            pe.wait_ge(S["ret_a_split"], h * 4 + (jt + 1))
                        m = 512 - 128 * jt
                        end = mm3(o[:, 128 * jt:512], VH[:, jt, vs], VL[:, jt, vs], AH[:, jt, 0:m], AL[:, jt, 0:m],
                                  jt == 0, jt == NT - 1)
                    end.then_inc(S["ret_o_made"], 1)
                w = panel(n + 5, 1)
                end = tile_of(bank(2)[:, :], w, 0, 256, HH, HL, 0, KD)
                end.then_inc(S["ret_g_made"], 1)
                o = bank(4)
                pe.wait_ge(S["ret_squares"], h + 1)
                nc.tensor.matmul(o[:, :], ONES[:, :], SS[:, :], start=True, stop=True).then_inc(S["ret_sum"], 1)
                end = tile_of(bank(3)[:, :], w, 1, 256, HH, HL, 0, KD)
                end.then_inc(panel_used, 1)
                for j in range(2):
                    w = panel(n + 6 + j, j % 2)
                    for f in range(4):
                        end = tile_of(bank(f)[:, :], w, f, 512, YH, YL, 0, 4,
                                      wait=(lambda k: pe.wait_ge(S["ret_y_split"], h * 4 + (k + 1))) if j + f == 0 else None)
                        signal(end, "ret_out_made", f == 3)
            uses.end(RET_HEADS)

            def per_layer_input(L, n):
                w = panel(n, n % 2)
                for f in range(KD):
                    end = tile_of(bank(f % 4)[:, :], w, f, 1024, PH, PL, 0, 2,
                                  wait=(lambda k: pe.wait_ge(S["ple_p_split"], 2 * L + k + 1)) if f == 0 else None)
                    signal(end, "ple_proj_made", f == KD - 1)
                    if f == 3:
                        sum_of_squares(f"post{L}")
                for j in range(4):
                    w = panel(n + 1 + j, (n + 1 + j) % 2)
                    for f in range(2):
                        end = tile_of(bank((2 * j + f) % 4)[:, :], w, f, 256, HH, HL, 0, KD,
                                      wait=(lambda k: pe.wait_ge(S["ple_h_split"], KD * L + k + 1)) if j + f == 0 else None)
                        signal(end, "ple_gate_made", f == 1)

            per_layer_input(0, N_PLE0)

            sum_of_squares("pre1")
            for j in range(5):
                n = N_MLAIN + j
                w = panel(n, n % 2)
                for f in range(2):
                    end = tile_of(bank((2 * j + f) % 4)[:, :], w, f, 256, HH, HL, 0, KD,
                                  wait=of_h("pre1") if j + f == 0 else None)
                    signal(end, "mla_in_made", f == 1)
                if j == 3:
                    sum_of_squares("cq")
            sum_of_squares("ckv", TG[:, 0, :])

            with pe.Fori(0, PAIRS) as hp:
                uses.loop(hp, [5] * 4 + [4] * 4)
                n = hp * 4 + N_MLA
                s0, s1 = N_MLA % 2, (N_MLA + 1) % 2
                w = panel(n, s0)
                pe.wait_ge(S["latent_split"], KQ)
                for f in range(2):
                    tile_of(bank(f)[:, :], w, f, 256, CQH, CQL, 0, KQ).then_inc(S["mla_qk_made"], 1)
                pe.wait_ge(S["latent_split"], KQ + KC)
                for f in range(2):
                    end = tile_of(bank(2 + f)[:, :], w, f, 256, CKH, CKL, 0, KC, at=KQ * 256)
                    signal(end, "mla_qk_made", f == 1)
                w = panel(n + 1, s1)
                for f in range(2):
                    tile_of(bank(f)[:, :], w, f, 256, CQH, CQL, 0, KQ).then_inc(S["mla_qr_made"], 1)
                wh, wl = w
                for j in range(2):
                    o = bank(2 + j)
                    for t2 in range(2):
                        ts = slice(256 * j + 128 * t2, 256 * j + 128 * t2 + 128)
                        for k in range(KC):
                            c = KQ * 256 + 256 * k
                            end = mm3(o[:, 256 * t2:256 * t2 + 256], CKH[:, k, ts], CKL[:, k, ts],
                                      wh[:, c:c + 256], wl[:, c:c + 256], k == 0, k == KC - 1)
                    signal(end, "mla_v_made", j == 1)

                def scores(a):
                    rows = slice(64 * a, 64 * a + 64)
                    for qt in range(NT):
                        o, m = bank(4 + qt)[:, 0:128 * (qt + 1)], 128 * (qt + 1)
                        qs = slice(128 * qt, 128 * qt + 128)
                        mm3(o, MQH[:, a, qs], MQL[:, a, qs], MQH[:, 2 + a, 0:m], MQL[:, 2 + a, 0:m], True, False)
                        mm3(o, QRH[rows, qs], QRL[rows, qs], KRH[rows, 0:m], KRL[rows, 0:m], False, True)\
                            .then_inc(S["mla_s_made"], 1)

                def transposes(a):
                    for qt in range(NT):
                        pe.wait_ge(S["mla_p_ready"], hp * 8 + (4 * a + qt + 1))
                        o = bank(4 + qt)
                        for jt in range(qt + 1):
                            end = nc.tensor.transpose(o[:, 128 * jt:128 * jt + 128], T[:, qt, 128 * jt:128 * jt + 128], IDENT)
                        end.then_inc(S["mla_t_made"], 1)

                def weighted(a):
                    o = bank(2 + a)
                    vs = slice(128 * a, 128 * a + 128)
                    for qt in range(NT):
                        pe.wait_ge(S["mla_pt_split"], hp * 8 + (4 * a + qt + 1))
                        for jt in range(qt + 1):
                            c = 128 * (qt * (qt + 1) // 2 + jt)
                            end = mm3(o[:, 128 * qt:128 * qt + 128], MVH[:, jt, vs], MVL[:, jt, vs],
                                      PKH[:, c:c + 128], PKL[:, c:c + 128], jt == 0, jt == qt)
                    end.then_inc(S["mla_o_made"], 1)

                pe.wait_ge(S["mla_qk_split"], hp * 4 + 4)
                pe.wait_ge(S["mla_rope_split"], hp + 2)
                scores(0)
                w = panel(n + 2, s0)
                tile_of(bank(0)[:, :], w, 0, 256, HH, HL, 0, KD).then_inc(S["mla_g_made"], 1)
                transposes(0)
                scores(1)
                pe.wait_ge(S["mla_v_split"], hp * 2 + 2)
                weighted(0)
                end = tile_of(bank(1)[:, :], w, 1, 256, HH, HL, 0, KD)
                end.then_inc(panel_used, 1)
                transposes(1)
                weighted(1)
                w = panel(n + 3, s1)
                for f in range(KD):
                    end = tile_of(bank(f % 4)[:, :], w, f, 1024, MYH, MYL, 0, 2,
                                  wait=(lambda k: pe.wait_ge(S["mla_y_split"], hp * 2 + (k + 1))) if f == 0 else None)
                    signal(end, "mla_out_made", f == KD - 1)
            uses.end(PAIRS)

            per_layer_input(1, N_PLE1)

            sum_of_squares("mix0")
            for cc in range(2):
                os_ = [bank(4 * cc + tt) for tt in range(NT)]
                for j in range(2):
                    n = N_MIX + 2 * cc + j
                    wh, wl = panel(n, n % 2)
                    for tt in range(NT):
                        ts = slice(128 * tt, 128 * tt + 128)
                        for k in range(4):
                            if cc == 0 and tt == 0:
                                of_h("mix0")(4 * j + k)
                            end = mm3(os_[tt][:, :], HH[:, 4 * j + k, ts], HL[:, 4 * j + k, ts],
                                      wh[:, 512 * k:512 * k + 512], wl[:, 512 * k:512 * k + 512],
                                      j == 0 and k == 0, j == 1 and k == 3)
                        if j == 1 or tt == NT - 1:
                            signal(end, "mix_v_made", tt == NT - 1)
            for j in range(4):
                n = N_MIX + 4 + j
                w = panel(n, n % 2)
                for f in range(2):
                    end = tile_of(bank((2 * j + f) % 4)[:, :], w, f, 256, HH, HL, 0, KD)
                    signal(end, "mix_u_made", f == 1)
            pe.wait_ge(S["wt_masked"], 1)
            for j in range(2):
                nc.tensor.matmul(bank(4 + j)[:, :], ONES[:, :], WT[:, 4 * j:4 * j + 4, :].rearrange("p g t -> p (g t)"),
                                 start=True, stop=True).then_inc(S["rowsum_made"], 1)
            pe.wait_ge(S["wt_split"], 1)
            pe.wait_ge(S["mix_split"], NT)
            for g in range(GROUPS):
                o = bank(g % 4)
                for tt in range(NT):
                    gs = slice(128 * g, 128 * g + 128)
                    end = mm3(o[:, 128 * tt:128 * tt + 128], NVH[:, tt, gs], NVL[:, tt, gs], WTH[:, g, :], WTL[:, g, :],
                              True, True)
                end.then_inc(S["mixed"], 1)
            YMH = NVH[:, :, :].rearrange("p t (g c) -> p g t c", g=GROUPS)
            YML = NVL[:, :, :].rearrange("p t (g c) -> p g t c", g=GROUPS)
            for j in range(4):
                n = N_MIX + 8 + j
                wh, wl = panel(n, n % 2)
                for f in range(2):
                    o = bank((2 * j + f) % 4)
                    for g in range(GROUPS):
                        if j + f == 0:
                            pe.wait_ge(S["mix_split"], NT + g + 1)
                        c = 256 * g + 128 * f
                        end = mm3(o[:, :], wh[:, c:c + 128], wl[:, c:c + 128], YMH[:, g], YML[:, g],
                                  g == 0, g == GROUPS - 1)
                    signal(end, "mix_out_made", f == 1)

            def mlp(L, n0):
                name = f"mlp{L}"
                sum_of_squares(name)
                with pe.Fori(0, CHUNKS) as c:
                    uses.loop(c, [2] * 4 + [1] * 4)
                    n = c * 4 + n0
                    for j in range(2):
                        w = panel(n + j, (n0 + j) % 2)
                        for f in range(2):
                            end = tile_of(bank(2 * j + f)[:, :], w, f, 256, HH, HL, 0, KD,
                                          wait=of_h(name) if j + f == 0 else None)
                            signal(end, "mlp_up_made", f == 1)
                    for j in range(2):
                        w = panel(n + 2 + j, (n0 + j) % 2)
                        for f in range(4):
                            end = tile_of(bank(4 * (1 - j) + f)[:, :], w, f, 512, HIDH, HIDL, 0, 4,
                                          wait=(lambda k: pe.wait_ge(S["mlp_hid_split"], c * 4 + (4 * CHUNKS * L + k + 1)))
                                          if j + f == 0 else None)
                            signal(end, "mlp_down_made", f == 3)
                uses.end(CHUNKS)

            mlp(0, N_MLP0)

            sum_of_squares("mix1")
            for half in range(2):
                for g, dil in enumerate(DILATIONS):
                    u = 3 * half + g
                    for j in range(2):
                        n = N_DIL + 3 * u + j
                        w = panel(n, n % 2)
                        for f in range(2):
                            end = tile_of(bank(2 * j + f)[:, :], w, f, 256, HH, HL, 0, KD,
                                          wait=of_h("mix1") if u + j + f == 0 else None)
                            signal(end, "dil_qk_made", f == 1)
                    n = N_DIL + 3 * u + 2
                    wh, wl = panel(n, n % 2)
                    for j in range(2):
                        o = bank(j)
                        for t2 in range(2):
                            tt = 2 * j + t2
                            if g == 0:
                                hs = [x[:, :, 128 * tt:128 * tt + 128] for x in (HH, HL)]
                            else:
                                hs = [x[:, :, :].rearrange("p k (a r) -> p k r a", r=4)[:, :, tt, :] for x in (HH, HL)]
                            for k in range(KD):
                                end = mm3(o[:, 256 * t2:256 * t2 + 256], hs[0][:, k], hs[1][:, k],
                                          wh[:, 256 * k:256 * k + 256], wl[:, 256 * k:256 * k + 256],
                                          k == 0, k == KD - 1)
                        signal(end, "dil_v_made", j == 1)
                    pe.wait_ge(S["dil_qk_split"], 4 * u + 4)
                    for hh in range(4):
                        pr, rows = hh // 2, slice(64 * (hh % 2), 64 * (hh % 2) + 64)
                        a = 4 * u + hh
                        o = bank(4)
                        for tt in range(NT):
                            ts = slice(128 * tt, 128 * tt + 128)
                            end = mm3(o[:, ts], DQH[rows, pr, ts], DQL[rows, pr, ts], DKH[rows, pr, ts], DKL[rows, pr, ts],
                                      True, True)
                        if g == 0:
                            o = bank(5)
                            for tt in range(1, NT):
                                ts, ps = slice(128 * tt, 128 * tt + 128), slice(128 * tt - 128, 128 * tt)
                                end = mm3(o[:, ps], DQH[rows, pr, ts], DQL[rows, pr, ts], DKH[rows, pr, ps], DKL[rows, pr, ps],
                                          True, True)
                        end.then_inc(S["dil_s_made"], 1)
                        pe.wait_ge(S["dil_p_ready"], a + 1)
                        o = bank(6)
                        for tt in range(NT):
                            ts = slice(128 * tt, 128 * tt + 128)
                            end = nc.tensor.transpose(o[:, ts], T[:, 0, ts], IDENT)
                        if g == 0:
                            o = bank(7)
                            for tt in range(1, NT):
                                ps = slice(128 * tt - 128, 128 * tt)
                                end = nc.tensor.transpose(o[:, ps], T[:, 1, ps], IDENT)
                        end.then_inc(S["dil_t_made"], 1)
                        pe.wait_ge(S["dil_v_split"], 2 * u + 2)
                        pe.wait_ge(S["dil_pt_split"], a + 1)
                        o = bank(2 + hh % 2)
                        vs = slice(128 * pr, 128 * pr + 128)
                        for tt in range(NT):
                            ts = slice(128 * tt, 128 * tt + 128)
                            both = g == 0 and tt > 0
                            end = mm3(o[:, ts], DVH[:, tt, vs], DVL[:, tt, vs], DPH[:, 0, ts], DPL[:, 0, ts], True, not both)
                            if both:
                                ps = slice(128 * tt - 128, 128 * tt)
                                end = mm3(o[:, ts], DVH[:, tt - 1, vs], DVL[:, tt - 1, vs], DPH[:, 1, ps], DPL[:, 1, ps],
                                          False, True)
                        end.then_inc(S["dil_o_made"], 1)
                for pr in range(2):
                    for g in range(3):
                        o = bank(4 + g)
                        for tt in range(NT):
                            if tt == 0:
                                pe.wait_ge(S["dil_lse"], 6 * half + 3 * pr + g + 1)
                            end = nc.tensor.matmul(o[:, 128 * tt:128 * tt + 128], LSE_COLS[g][:, 128 * tt:128 * tt + 128], IDENT,
                                                   start=True, stop=True)
                        end.then_inc(S["dil_lse_made"], 1)
            for j in range(2):
                n = N_DILOUT + j
                w = panel(n, n % 2)
                for f in range(4):
                    end = tile_of(bank(f)[:, :], w, f, 512, DYH, DYL, 0, 4,
                                  wait=(lambda k: pe.wait_ge(S["dil_y_split"], k + 1)) if j + f == 0 else None)
                    signal(end, "dil_out_made", f == 3)

            mlp(1, N_MLP1)
            sum_of_squares("final")

        @block.scalar
        def _(act):
            def hi(dst, src):
                return nc.scalar.activation(dst, src, ACT.Copy)

            def split_panel(m, slot, half):
                act.wait_ge(raw_loaded[slot], half * 16 + 16)
                if not isinstance(m, int) or m >= 2:
                    act.wait_ge(panel_used, m - 1)
                hi(WH[:, slot, :], RAW[:, slot, :]).then_inc(hi_ready, 1)

            def split_at(m):
                split_panel(m, m % 2, m // 2)

            def split_in(i, per, m0):
                split_panel(i * per + m0, m0 % 2, i * (per // 2) + m0 // 2)

            def squares(name, n, ready):
                for k in range(n):
                    src = ready(k)
                    if k == 0:
                        nc.scalar.activation(SS[:, :], src, ACT.Square).then_inc(S["norm_sq"], 1)
                        continue
                    if k >= 3:
                        act.wait_ge(S["norm_added"], (KD - 1) * FULL.index(name) + k - 2)
                    nc.scalar.activation(SQ[:, k % 2, :], src, ACT.Square).then_inc(S["norm_sq"], 1)

            def root(name, n):
                act.wait_ge(S["norm_sum"], NORMS.index(name) + 1)
                nc.scalar.activation(R[:, :], B[4][:, :], ACT.Sqrt, bias=EPSC[:, 0:1], scale=1.0 / n)\
                    .then_inc(S["norm_root"], 1)

            def split_h(name, n, dh, before=0):
                for k in range(n):
                    act.wait_ge(S[name + "_f32"], before + k + 1)
                    hi(dh[:, k, :], T[:, k % 2, :]).then_inc(S[name + "_hi"], 1)

            def norm(name, ready):
                squares(name, KD, ready)
                root(name, D_MODEL)
                split_h("norm", KD, HH, KD * SPLIT.index(name))

            act.dma_start(X[:, :, :], xin.rearrange("k p n -> p k n")).then_inc(S["x_moved"], 16)
            act.dma_start(G[:, :], gains).then_inc(S["const_loaded"], 16)
            act.dma_start(CONST[:, :], consts).then_inc(S["const_loaded"], 16)
            act.dma_start(SIN1[:, :].bitcast(i32), pos).then_inc(S["pos_loaded"], 16)
            act.dma_start(REL[0:32], rel).then_inc(S["rel_loaded"], 16)
            act.dma_start(ONEHOT, onehot.rearrange("b (j n) -> b j n", j=2)).then_inc(S["rel_loaded"], 16)
            split_at(0)
            act.wait_ge(S["x_moved"], 16)
            for j in range(2):
                act.wait_ge(S["bias_rows"], j + 1)
                hi(ROWS[:, j, :], B[5 + j][0:24, :]).then_inc(free[5 + j], 1)
                act.wait_ge(free[5 + j], 1)
            for kind in range(4):
                g = kind % 3
                src = ROWS8[g][:, kind // 2, 256 * (kind % 2):256 * (kind % 2) + 256]
                act.dma_start(scratch[kind], src.unsqueeze(1).to_broadcast([8, 128, 256])).then_inc(S["rows_stored"], 16)
            norm("pre0", lambda k: X[:, k, :])
            for j, dst in enumerate((COS1, SIN1)):
                act.wait_ge(S["angle"], j + 1)
                nc.scalar.activation(dst[:, :], T[:, 2 + j, :], ACT.Sin).then_inc(S["sines"], 1)

            split_at(1)
            with act.Fori(0, RET_HEADS) as h:
                hs = act.snap(h * 1)
                act.dma_start(DEC[:, :], decay[bass.ds(hs, 1)].rearrange("a p n -> (a p) n")).then_inc(S["head_loaded"], 16)
                act.dma_start(GN[:, :], gn[bass.ds(hs, 1)].rearrange("a p n -> (a p) n")).then_inc(S["head_loaded"], 16)
                for j, dst in enumerate((QH, KH)):
                    for f in range(2):
                        act.wait_ge(S["ret_qk_f32"], h * 4 + (2 * j + f + 1))
                        hi(dst[:, f, :], T[:, 2 * f, :]).then_inc(S["ret_qk_hi"], 1)
                    split_in(h, 8, 2 + j)
                split_in(h, 8, 4)
                for tt in range(NT):
                    tile_done(act, "ret_v_made", tt, 4, h * 8 + 3, h * 3)
                    hi(VH[:, tt, :], B[tt][:, :]).then_inc(S["ret_v_hi"], 1)
                split_in(h, 8, 5)
                for jt in range(NT):
                    act.wait_ge(S["ret_a_f32"], h * 4 + (jt + 1))
                    m = 512 - 128 * jt
                    hi(AH[:, jt, 0:m], T[:, jt, 0:m]).then_inc(S["ret_a_hi"], 1)
                for f in range(2):
                    tile_done(act, "ret_g_made", f, 2, h * 8 + 4, h * 2)
                    nc.scalar.activation(TG[:, f, :], B[f][:, :], ACT.Tanh, scale=0.5).then_inc(S["ret_tanh"], 1)
                split_in(h, 8, 6)
                for vt in range(4):
                    act.wait_ge(S["ret_o_made"], h * 4 + (vt + 1))
                    if vt == 0:
                        dst = SS[:, :]
                    else:
                        dst = SQ[:, vt % 2, :]
                    if vt == 3:
                        act.wait_ge(S["ret_added"], h * 3 + 1)
                    nc.scalar.activation(dst, B[4 + vt][:, :], ACT.Square).then_inc(S["ret_sq"], 1)
                tile_done(act, "ret_g_made", 2, 2, h * 8 + 5, h * 2)
                act.wait_ge(S["ret_u"], h * 4 + 1)
                nc.scalar.activation(TG[:, 0, :], B[2][:, :], ACT.Tanh, scale=0.5).then_inc(S["ret_tanh"], 1)
                act.wait_ge(S["ret_sum"], h + 1)
                nc.scalar.activation(R[:, :], B[4][:, :], ACT.Sqrt, bias=EPSC[:, 1:2], scale=4.0 / RET_V)\
                    .then_inc(S["ret_root"], 1)
                tile_done(act, "ret_g_made", 3, 2, h * 8 + 5, h * 2)
                act.wait_ge(S["ret_u"], h * 4 + 2)
                nc.scalar.activation(TG[:, 1, :], B[3][:, :], ACT.Tanh, scale=0.5).then_inc(S["ret_tanh"], 1)
                split_in(h, 8, 7)
                for vt in range(4):
                    act.wait_ge(S["ret_y_f32"], h * 4 + (vt + 1))
                    hi(YH[:, vt, :], O[:, vt, :]).then_inc(S["ret_y_hi"], 1)
                split_in(h, 8, 8)
                split_in(h, 8, 9)

            def per_layer_input(L, n):
                act.wait_ge(S["ple_begin"], L + 1)
                act.dma_start(PF[:, :, :], pin[L].rearrange("k p n -> p k n")).then_inc(S["p_loaded"], 16)
                act.wait_ge(S["p_loaded"], 16 * L + 16)
                for k in range(2):
                    hi(PH[:, k, :], PF[:, k, :]).then_inc(S["ple_p_hi"], 1)
                if L == 1:
                    split_at(n + 1)
                squares(f"post{L}", KD, lambda k: ACC[:, k, :])
                for f in range(KD):
                    tile_done(act, "ple_proj_made", f, KD, n, base=7 * L)
                    hi(PJ[:, f, :], B[f % 4][:, :]).then_inc(free[f % 4], 1)
                    if f == 3:
                        root(f"post{L}", D_MODEL)
                for k in range(KD):
                    act.wait_ge(S["ple_x_new"], KD * L + k + 1)
                    hi(HH[:, k, :], X[:, k, :]).then_inc(S["ple_hi"], 1)
                for f in range(KD):
                    if f % 2 == 0:
                        split_at(n + 2 + f // 2)
                    tile_done(act, "ple_gate_made", f, 2, n + 1 + f // 2, base=4 * L)
                    if f >= 2:
                        act.wait_ge(S["ple_mixed"], KD * L + f - 1)
                    nc.scalar.activation(TG[:, f % 2, :], B[f % 4][:, :], ACT.Tanh, scale=0.5).then_inc(S["ple_tanh"], 1)

            def updated(sig, before=0):
                def ready(k):
                    act.wait_ge(S[sig], before + k + 1)
                    return X[:, k, :]
                return ready

            per_layer_input(0, N_PLE0)
            norm("pre1", updated("ple_done"))
            act.dma_start(xsave.rearrange("k p n -> p k n"), X[:, :, :]).then_inc(S["x_moved"], 16)
            act.wait_ge(S["x_moved"], 32)
            act.dma_start(SIN2[:, :].bitcast(i32), pos).then_inc(S["pos_loaded"], 16)
            split_at(N_MLAIN + 1)
            for f in range(KQ + KC):
                tile_done(act, "mla_in_made", f, 2, N_MLAIN + f // 2)
                hi(ACC[:, f, :], B[f % 4][:, :])
                if f >= KQ:
                    dst = TG[:, f - KQ, :]
                elif f == 0:
                    dst = SS[:, :]
                else:
                    dst = SQ[:, f % 2, :]
                    if f >= 3:
                        act.wait_ge(S["cq_added"], f - 2)
                nc.scalar.activation(dst, B[f % 4][:, :], ACT.Square).then_inc(S["mla_sq"], 1)
                act.drain().then_inc(free[f % 4], 1)
                if f % 2 == 1:
                    split_at(N_MLAIN + 2 + f // 2)
            for j, dst in enumerate((COS2, SIN2)):
                act.wait_ge(S["angle"], j + 3)
                nc.scalar.activation(dst[:, :], T[:, 2 + j, :], ACT.Sin).then_inc(S["sines"], 1)
            root("cq", Q_LORA)
            split_h("latent", KQ, CQH)
            act.wait_ge(S["mla_rope_f32"], 1)
            hi(KRH[:, :], T[:, 2, :]).then_inc(S["mla_rope_hi"], 1)
            root("ckv", KV_LORA)
            split_h("latent", KC, CKH, KQ)

            with act.Fori(0, PAIRS) as hp:
                split_in(hp, 4, N_MLA + 1)
                for f in range(4):
                    tile_done(act, "mla_qk_made", f, 4, hp * 4 + N_MLA, hp * 3)
                    hi(MQH[:, f, :], B[f][:, :]).then_inc(S["mla_qk_hi"], 1)
                split_in(hp, 4, N_MLA + 2)
                act.wait_ge(S["mla_rope_f32"], hp + 2)
                hi(QRH[:, :], T[:, 0, :]).then_inc(S["mla_rope_hi"], 1)
                for j in range(2):
                    tile_done(act, "mla_v_made", j, 2, hp * 4 + (N_MLA + 1), hp * 1)
                    hi(MVH[:, 2 * j:2 * j + 2, :].rearrange("p t n -> p (t n)"), B[2 + j][:, :]).then_inc(S["mla_v_hi"], 1)
                split_in(hp, 4, N_MLA + 3)

                def exponentials(a):
                    for qt in range(NT):
                        m = 128 * (qt + 1)
                        act.wait_ge(S["mla_max"], hp * 2 + (a + 1))
                        if a == 1:
                            act.wait_ge(S["mla_t_made"], hp * 8 + (qt + 1))
                        nc.scalar.activation(T[:, qt, 0:m], B[4 + qt][:, 0:m], ACT.Exp, bias=ST[:, 1, qt:qt + 1],
                                             scale=MLA_SCALE, accum_out=ST[:, 2, qt:qt + 1]).then_inc(S["mla_exp"], 1)

                def high_probabilities(a):
                    for qt in range(NT):
                        act.wait_ge(S["mla_t_made"], hp * 8 + (4 * a + qt + 1))
                        c, m = 128 * (qt * (qt + 1) // 2), 128 * (qt + 1)
                        hi(PKH[:, c:c + m], B[4 + qt][:, 0:m]).then_inc(S["mla_pt_hi"], 1)

                def tanh_gate(a):
                    tile_done(act, "mla_g_made", a, 2, hp * 4 + (N_MLA + 2), hp * 1)
                    nc.scalar.activation(TG[:, a, :], B[a][:, :], ACT.Tanh, scale=0.5).then_inc(S["mla_tanh"], 1)

                def high_y(a):
                    act.wait_ge(S["mla_y_f32"], hp * 2 + (a + 1))
                    hi(MYH[:, a, :], SQ[:, a, :]).then_inc(S["mla_y_hi"], 1)

                exponentials(0)
                tanh_gate(0)
                high_probabilities(0)
                exponentials(1)
                high_y(0)
                tanh_gate(1)
                high_probabilities(1)
                high_y(1)
                split_in(hp, 4, N_MLA + 4)

            act.wait_ge(S["ple_begin"], 2)
            act.dma_start(X[:, :, :], xsave.rearrange("k p n -> p k n")).then_inc(S["x_moved"], 16)
            per_layer_input(1, N_PLE1)
            norm("mix0", updated("ple_done", KD))

            act.dma_start(WT[:, :, :], wsT).then_inc(S["ws_loaded"], 16)
            act.dma_start(BS[:, :, :], bs).then_inc(S["ws_loaded"], 16)
            split_at(N_MIX + 1)
            for cc in range(2):
                split_at(N_MIX + 2 + 2 * cc)
                for tt in range(NT):
                    tile_done(act, "mix_v_made", 4 * cc + tt, 4, N_MIX + 2 * cc + 1)
                    nc.scalar.activation(NV[:, tt, 512 * cc:512 * cc + 512], B[4 * cc + tt][:, :], ACT.Gelu,
                                         accum_out=ST[:, cc, tt:tt + 1]).then_inc(free[4 * cc + tt], 1)
                    act.drain().then_inc(S["mix_gelu"], 1)
                split_at(N_MIX + 3 + 2 * cc)
            for tt in range(NT):
                act.drain()
                act.wait_ge(S["nv_centred"], tt + 1)
                nc.scalar.activation(SQ[:, :, :].rearrange("p a n -> p (a n)"), NV[:, tt, :], ACT.Square,
                                     accum_out=ST[:, 4, tt:tt + 1]).then_inc(S["nv_var"], 1)
            act.wait_ge(S["nv_var"], NT)
            nc.scalar.activation(ST[:, 5, :], ST[:, 4, :], ACT.Sqrt, bias=EPSC[:, 0:1], scale=1.0 / 1024)\
                .then_inc(S["nv_root"], 1)
            for tt in range(NT):
                act.wait_ge(S["mix_f32"], tt + 1)
                hi(NVH[:, tt, :], NV[:, tt, :]).then_inc(S["mix_hi"], 1)
            act.wait_ge(S["wt_masked"], 1)
            hi(WTH[:, :, :], WT[:, :, :]).then_inc(S["wt_hi"], 1)
            for f in range(8):
                tile_done(act, "mix_u_made", f, 2, N_MIX + 4 + f // 2)
                nc.scalar.activation(GU[:, f, :], B[f % 4][:, :], ACT.Gelu).then_inc(free[f % 4], 1)
                if f % 2 == 1 and f < 7:
                    split_at(N_MIX + 6 + f // 2)
            act.drain().then_inc(S["mix_u"], 1)
            split_at(N_MIX + 9)
            for g in range(GROUPS):
                act.wait_ge(S["mix_f32"], NT + g + 1)
                hi(NVH[:, :, 128 * g:128 * g + 128], T[:, g % 2, :].rearrange("p (t n) -> p t n", t=NT))\
                    .then_inc(S["mix_hi"], 1)
            for j in range(3):
                split_at(N_MIX + 10 + j)

            def mlp(L, n0):
                at = 4 * CHUNKS * L

                def chunk(c, next_panel=True):
                    split_in(c, 4, n0 + 1)
                    for j in range(2):
                        for f in range(2 * j, 2 * j + 2):
                            tile_done(act, "mlp_up_made", f, 2, c * 4 + (n0 + f // 2), c * 2, 2 * CHUNKS * L)
                            if f >= 2:
                                act.wait_ge(S["mlp_hid_f32"], c * 4 + (at + f - 1))
                            nc.scalar.activation(TG[:, f % 2, :], B[f][:, :], ACT.Relu).then_inc(S["mlp_relu"], 1)
                            act.drain().then_inc(free[f], 1)
                        for f in range(2 * j, 2 * j + 2):
                            act.wait_ge(S["mlp_hid_f32"], c * 4 + (at + f + 1))
                            hi(HIDH[:, f, :], T[:, f, :]).then_inc(S["mlp_hid_hi"], 1)
                        split_in(c, 4, n0 + 2 + j)
                    if next_panel:
                        split_in(c, 4, n0 + 4)

                if L == 0:
                    with act.Fori(0, CHUNKS) as c:
                        chunk(c)
                else:
                    with act.Fori(0, CHUNKS - 1) as c:
                        chunk(c)
                    chunk(CHUNKS - 1, next_panel=False)

            norm("mlp0", updated("mix_done"))
            mlp(0, N_MLP0)

            norm("mix1", updated("mlp_done"))
            act.wait_ge(S["rows_stored"], 64)
            for kind in range(4):
                rows = scratch[kind].rearrange("h q y -> h (q y)")[:, 127:127 + 128 * 255]
                tile = rows.rearrange("h (q y) -> q h y", y=255)[:, :, 0:128]
                act.dma_start(TAB[:, kind], tile).then_inc(S["tab_loaded"], 16)
            for half in range(2):
                for g in range(3):
                    u = 3 * half + g
                    n = N_DIL + 3 * u
                    split_at(n + 1)
                    for f in range(4):
                        tile_done(act, "dil_qk_made", f, 2, n + f // 2, 2 * u)
                        dst = (DQH if f < 2 else DKH)[:, f % 2, :]
                        hi(in_order(dst, g), natural(B[f], g)).then_inc(S["dil_qk_hi"], 1)
                        if f == 1:
                            split_at(n + 2)
                    split_at(n + 3)
                    for j in range(2):
                        tile_done(act, "dil_v_made", j, 2, n + 2, u)
                        hi(DVH[:, 2 * j:2 * j + 2, :].rearrange("p t n -> p (t n)"), B[j][:, :]).then_inc(S["dil_v_hi"], 1)
                    for hh in range(4):
                        a = 4 * u + hh
                        act.wait_ge(S["dil_centred"], a + 1)
                        nc.scalar.activation(T[:, 0, :], T[:, 0, :], ACT.Exp)
                        if g == 0:
                            nc.scalar.activation(T[:, 1, 0:384], T[:, 1, 0:384], ACT.Exp)
                        act.drain().then_inc(S["dil_exp"], 1)
                        act.wait_ge(S["dil_t_made"], a + 1)
                        hi(DPH[:, 0, :], B[6][:, :])
                        if g == 0:
                            hi(DPH[:, 1, 0:384], B[7][:, 0:384])
                        act.drain().then_inc(S["dil_pt_hi"], 1)
                        act.wait_ge(S["dil_o_made"], a + 1)
                        rows = slice(64 * (hh % 2), 64 * (hh % 2) + 64)
                        hi(natural(OG[hh // 2][rows, g, :], g), in_order(B[2 + hh % 2][rows, :], g)).then_inc(free[2 + hh % 2], 1)
                act.wait_ge(S["dil_sums"], half + 1)
                nc.scalar.activation(SUMS[:, :, :, :].rearrange("p a b c -> p (a b c)"),
                                     SUMS[:, :, :, :].rearrange("p a b c -> p (a b c)"), ACT.Ln).then_inc(S["dil_ln"], 1)
                for pr in range(2):
                    v = 2 * half + pr
                    for g in range(3):
                        act.wait_ge(S["dil_lse_made"], 3 * v + g + 1)
                        hi(natural(LSE[:, g, :], g), in_order(B[4 + g][:, :], g)).then_inc(free[4 + g], 1)
                    act.drain().then_inc(S["dil_lse_copied"], 1)
                    act.wait_ge(S["dil_lse_centred"], v + 1)
                    nc.scalar.activation(LSE, LSE, ACT.Exp).then_inc(S["dil_weights"], 1)
                    act.wait_ge(S["dil_y_f32"], v + 1)
                    hi(DYH[:, v, :], DY).then_inc(S["dil_y_hi"], 1)
            for j in range(2):
                split_at(N_DILOUT + 1 + j)
            norm("mlp1", updated("dil_done"))
            mlp(1, N_MLP1)
            squares("final", KD, updated("mlp_done", KD))
            root("final", D_MODEL)

        @block.vector
        def _(ve):
            v = nc.vector

            def lo(dst, src, high):
                return v.tensor_tensor(dst, src, high.bitcast(f32), ALU.subtract)

            def gain(name, k):
                c = GAIN_AT[name] + k
                return G[:, c:c + 1]

            def add_squares(name, n):
                for k in range(1, n):
                    ve.wait_ge(S["norm_sq"], n * FULL.index(name) + k + 1)
                    if k > 1:
                        ve.drain()
                    v.tensor_tensor(SS[:, :], SS[:, :], SQ[:, k % 2, :], ALU.add).then_inc(S["norm_added"], 1)
                ve.drain().then_inc(S["norm_squares"], 1)

            def inverse_root(name):
                ve.wait_ge(S["norm_root"], NORMS.index(name) + 1)
                v.reciprocal(R[:, :], R[:, :]).then_inc(free[4], 1)
                ve.drain()

            def scaled(name, n, src, gains_of, dh, dl, sig, before=0):
                for k in range(n + 1):
                    if k < n:
                        ve.drain()
                        v.scalar_tensor_tensor(T[:, k % 2, :], src[:, k, :], gain(gains_of[0], gains_of[1] + k), R[:, :],
                                               ALU.mult, ALU.mult).then_inc(S[name + "_f32"], 1)
                    if k > 0:
                        ve.wait_ge(S[name + "_hi"], before + k)
                        lo(dl[:, k - 1, :], T[:, (k - 1) % 2, :], dh[:, k - 1, :]).then_inc(S[sig], 1)

            def norm(name):
                add_squares(name, KD)
                inverse_root(name)
                scaled("norm", KD, X, (name, 0), HH, HL, "norm_h_split", KD * SPLIT.index(name))

            def angles(use, positions, freq):
                t = [T[:, j, :] for j in range(4)]
                MAGIC = 1.5 * 2.0 ** 23
                ve.drain()
                ve.wait_ge(S["pos_loaded"], 16 * use)
                v.tensor_scalar(t[0], positions, freq, None, ALU.mult)

                def less(dst, src, per_turn, shift, parts):
                    ve.drain()
                    v.tensor_scalar(t[1], src, per_turn, shift, ALU.mult, ALU.add)
                    ve.drain()
                    v.tensor_scalar(t[1], t[1], MAGIC, MAGIC, ALU.add, ALU.subtract)
                    for part in parts:
                        ve.drain()
                        v.scalar_tensor_tensor(dst, t[1], -part, src, ALU.mult, ALU.add)
                        src = dst
                    ve.drain()

                turns = TWO_PI * COARSE
                less(t[0], t[0], 1.0 / turns, 0.0, _parts(turns, 7, 6))
                for dst, quarter in ((t[2], 0.25), (t[3], 0.0)):
                    less(dst, t[0], 1.0 / TWO_PI, quarter, _parts(TWO_PI, 8, 5))
                    v.tensor_scalar(dst, dst, quarter * TWO_PI, 3.1415925, ALU.add, ALU.min)
                    ve.drain()
                    v.tensor_scalar(dst, dst, -3.1415925, None, ALU.max).then_inc(S["angle"], 1)

            for b in BankUses.GIVEN:
                ve.drain().then_inc(free[b], 1)
            v.memset(ONES[:, :], 1.0)
            v.memset(EPSC[:, 0:1], EPS)
            v.memset(EPSC[:, 1:2], 4 * EPS)
            v.memset(REL[32:33, :], NEG)
            ve.drain().then_inc(S["rel_neg"], 1)
            ve.wait_ge(S["const_loaded"], 32)
            angles(1, SIN1[:, :].bitcast(i32), FREQ1)
            norm("pre0")
            ve.wait_ge(S["rows_stored"], 64)
            v.memset(ACC[:, :, :], 0.0)
            ve.wait_ge(S["sines"], 2)

            with ve.Fori(0, RET_HEADS) as h:
                for b, dh, dl in ((0, QH, QL), (2, KH, KL)):
                    ve.drain()
                    ve.wait_ge(panel_used, h * 8 + (1 + b // 2))
                    v.tensor_tensor(T[:, 0, :], B[b][:, :], COS1[:, :], ALU.mult)
                    v.tensor_tensor(T[:, 1, :], B[b + 1][:, :], SIN1[:, :], ALU.mult)
                    v.tensor_tensor(T[:, 2, :], B[b + 1][:, :], COS1[:, :], ALU.mult).then_inc(free[b + 1], 1)
                    v.tensor_tensor(T[:, 3, :], B[b][:, :], SIN1[:, :], ALU.mult).then_inc(free[b], 1)
                    ve.drain()
                    v.tensor_tensor(T[:, 0, :], T[:, 0, :], T[:, 1, :], ALU.subtract).then_inc(S["ret_qk_f32"], 1)
                    v.tensor_tensor(T[:, 2, :], T[:, 2, :], T[:, 3, :], ALU.add).then_inc(S["ret_qk_f32"], 1)
                    for f in range(2):
                        ve.wait_ge(S["ret_qk_hi"], h * 4 + (b + f + 1))
                        lo(dl[:, f, :], T[:, 2 * f, :], dh[:, f, :]).then_inc(S["ret_qk_split"], 1)
                for tt in range(NT):
                    ve.wait_ge(S["ret_v_hi"], h * 4 + (tt + 1))
                    lo(VL[:, tt, :], B[tt][:, :], VH[:, tt, :]).then_inc(S["ret_v_split"], 1)
                    ve.drain().then_inc(free[tt], 1)
                ve.drain()
                ve.wait_ge(S["head_loaded"], h * 32 + 32)
                for jt in range(NT):
                    m = 512 - 128 * jt
                    ve.wait_ge(S["ret_a_made"], h * 4 + (jt + 1))
                    v.tensor_tensor(T[:, jt, 0:m], B[4 + jt][:, 0:m], DEC[:, 0:m], ALU.mult).then_inc(S["ret_a_f32"], 1)
                    ve.drain().then_inc(free[4 + jt], 1)
                for jt in range(NT):
                    m = 512 - 128 * jt
                    ve.wait_ge(S["ret_a_hi"], h * 4 + (jt + 1))
                    lo(AL[:, jt, 0:m], T[:, jt, 0:m], AH[:, jt, 0:m]).then_inc(S["ret_a_split"], 1)

                def twice_silu(f):
                    ve.wait_ge(S["ret_tanh"], h * 4 + (f + 1))
                    v.scalar_tensor_tensor(U[:, f, :], TG[:, f % 2, :], 1.0, B[f][:, :], ALU.add, ALU.mult)\
                        .then_inc(S["ret_u"], 1)
                    ve.drain().then_inc(free[f], 1)

                twice_silu(0)
                twice_silu(1)
                for vt in range(4):
                    ve.wait_ge(S["ret_sq"], h * 4 + (vt + 1))
                    v.tensor_scalar(O[:, vt, :], B[4 + vt][:, :], GN[:, vt:vt + 1], None, ALU.mult).then_inc(free[4 + vt], 1)
                    if vt > 0:
                        v.tensor_tensor(SS[:, :], SS[:, :], SQ[:, vt % 2, :], ALU.add).then_inc(S["ret_added"], 1)
                        ve.drain()
                ve.drain().then_inc(S["ret_squares"], 1)
                for vt in range(2):
                    v.tensor_tensor(O[:, vt, :], O[:, vt, :], U[:, vt, :], ALU.mult)
                ve.drain()
                twice_silu(2)
                ve.wait_ge(S["ret_root"], h + 1)
                v.reciprocal(R[:, :], R[:, :]).then_inc(free[4], 1)
                ve.drain()
                for vt in range(2):
                    v.tensor_tensor(O[:, vt, :], O[:, vt, :], R[:, :], ALU.mult).then_inc(S["ret_y_f32"], 1)
                v.tensor_tensor(O[:, 2, :], O[:, 2, :], R[:, :], ALU.mult)
                v.tensor_tensor(O[:, 3, :], O[:, 3, :], R[:, :], ALU.mult)
                ve.drain()
                v.tensor_tensor(O[:, 2, :], O[:, 2, :], U[:, 2, :], ALU.mult).then_inc(S["ret_y_f32"], 1)
                twice_silu(3)
                v.tensor_tensor(O[:, 3, :], O[:, 3, :], U[:, 3, :], ALU.mult).then_inc(S["ret_y_f32"], 1)
                for vt in range(4):
                    ve.wait_ge(S["ret_y_hi"], h * 4 + (vt + 1))
                    lo(YL[:, vt, :], O[:, vt, :], YH[:, vt, :]).then_inc(S["ret_y_split"], 1)
                for f in range(KD):
                    tile_done(ve, "ret_out_made", f, 4, h * 8 + (6 + f // 4), h * 6)
                    v.tensor_tensor(ACC[:, f, :], ACC[:, f, :], B[f % 4][:, :], ALU.add).then_inc(free[f % 4], 1)

            def per_layer_input(L):
                post = f"post{L}"
                ve.drain().then_inc(S["ple_begin"], 1)
                for k in range(2):
                    ve.wait_ge(S["ple_p_hi"], 2 * L + k + 1)
                    lo(PL[:, k, :], PF[:, k, :], PH[:, k, :]).then_inc(S["ple_p_split"], 1)
                add_squares(post, KD)
                if L == 1:
                    ve.wait_ge(S["x_moved"], 48)
                inverse_root(post)
                for k in range(KD + 2):
                    if k < KD:
                        ve.drain()
                        v.scalar_tensor_tensor(T[:, k % 2, :], ACC[:, k, :], gain(post, k), R[:, :], ALU.mult, ALU.mult)
                        ve.drain()
                        v.tensor_tensor(X[:, k, :], X[:, k, :], T[:, k % 2, :], ALU.add).then_inc(S["ple_x_new"], 1)
                    if 0 < k <= KD:
                        ve.wait_ge(S["ple_hi"], KD * L + k)
                        lo(HL[:, k - 1, :], X[:, k - 1, :], HH[:, k - 1, :]).then_inc(S["ple_h_split"], 1)
                for f in range(KD):
                    ve.wait_ge(S["ple_tanh"], KD * L + f + 1)
                    ve.drain()
                    v.scalar_tensor_tensor(T[:, f % 2, :], TG[:, f % 2, :], 1.0, PJ[:, f, :], ALU.add, ALU.mult)\
                        .then_inc(S["ple_mixed"], 1)
                    ve.drain().then_inc(free[f % 4], 1)
                    v.scalar_tensor_tensor(X[:, f, :], T[:, f % 2, :], 0.5, X[:, f, :], ALU.mult, ALU.add)\
                        .then_inc(S["ple_done"], 1)

            per_layer_input(0)
            norm("pre1")

            angles(2, SIN2[:, :].bitcast(i32), FREQ2)
            for f in range(1, KQ):
                ve.wait_ge(S["mla_sq"], f + 1)
                if f > 1:
                    ve.drain()
                v.tensor_tensor(SS[:, :], SS[:, :], SQ[:, f % 2, :], ALU.add).then_inc(S["cq_added"], 1)
            ve.drain().then_inc(S["norm_squares"], 1)
            ve.wait_ge(S["mla_sq"], KQ + KC)
            v.tensor_tensor(TG[:, 0, :], TG[:, 0, :], TG[:, 1, :], ALU.add).then_inc(S["norm_squares"], 1)
            ve.wait_ge(S["sines"], 4)
            v.tensor_scalar(SIN2[:, :], SIN2[:, :], SIGN, None, ALU.mult)
            inverse_root("cq")
            scaled("latent", KQ, ACC, ("qn", 0), CQH, CQL, "latent_split")
            ve.wait_ge(panel_used, N_MLAIN + 5)
            v.tensor_tensor(T[:, 2, :], B[0][:, :], COS2[:, :], ALU.mult).then_inc(free[0], 1)
            v.tensor_tensor(T[:, 3, :], B[1][:, :], SIN2[:, :], ALU.mult).then_inc(free[1], 1)
            ve.drain()
            v.tensor_tensor(T[:, 2, :], T[:, 2, :], T[:, 3, :], ALU.add).then_inc(S["mla_rope_f32"], 1)
            ve.wait_ge(S["mla_rope_hi"], 1)
            lo(KRL[:, :], T[:, 2, :], KRH[:, :]).then_inc(S["mla_rope_split"], 1)
            inverse_root("ckv")
            scaled("latent", KC, ACC[:, KQ:KQ + KC, :], ("kvn", 0), CKH, CKL, "latent_split", KQ)
            v.memset(ACC[:, :, :], 0.0)
            ve.drain()

            with ve.Fori(0, PAIRS) as hp:
                for f in range(4):
                    ve.wait_ge(S["mla_qk_hi"], hp * 4 + (f + 1))
                    lo(MQL[:, f, :], B[f][:, :], MQH[:, f, :]).then_inc(S["mla_qk_split"], 1)
                    ve.drain().then_inc(free[f], 1)
                ve.drain()
                ve.wait_ge(S["mla_qr_made"], hp * 2 + 2)
                v.tensor_tensor(T[:, 0, :], B[0][:, :], COS2[:, :], ALU.mult).then_inc(free[0], 1)
                v.tensor_tensor(T[:, 1, :], B[1][:, :], SIN2[:, :], ALU.mult).then_inc(free[1], 1)
                ve.drain()
                v.tensor_tensor(T[:, 0, :], T[:, 0, :], T[:, 1, :], ALU.add).then_inc(S["mla_rope_f32"], 1)
                ve.wait_ge(S["mla_rope_hi"], hp + 2)
                lo(QRL[:, :], T[:, 0, :], QRH[:, :]).then_inc(S["mla_rope_split"], 1)
                for j in range(2):
                    ve.wait_ge(S["mla_v_hi"], hp * 2 + (j + 1))
                    vj = slice(2 * j, 2 * j + 2)
                    lo(MVL[:, vj, :].rearrange("p t n -> p (t n)"), B[2 + j][:, :],
                       MVH[:, vj, :].rearrange("p t n -> p (t n)")).then_inc(S["mla_v_split"], 1)
                    ve.drain().then_inc(free[2 + j], 1)

                def maxima(a):
                    for qt in range(NT):
                        ve.wait_ge(S["mla_s_made"], hp * 8 + (4 * a + qt + 1))
                        d = B[4 + qt][:, 128 * qt:128 * qt + 128]
                        v.tensor_tensor(d, d, CAUSAL, ALU.add)
                    ve.drain()
                    for qt in range(NT):
                        v.reduce_max(ST[:, 0, qt:qt + 1], B[4 + qt][:, 0:128 * (qt + 1)], AX.X)
                    ve.drain()
                    v.tensor_scalar(ST[:, 1, :], ST[:, 0, :], -MLA_SCALE, None, ALU.mult).then_inc(S["mla_max"], 1)

                def probabilities(a):
                    ve.wait_ge(S["mla_exp"], hp * 8 + (4 * a + 4))
                    v.reciprocal(ST[:, 3, :], ST[:, 2, :])
                    ve.drain()
                    for qt in range(NT):
                        m = 128 * (qt + 1)
                        v.tensor_scalar(T[:, qt, 0:m], T[:, qt, 0:m], ST[:, 3, qt:qt + 1], None, ALU.mult)\
                            .then_inc(S["mla_p_ready"], 1)
                        ve.drain().then_inc(free[4 + qt], 1)

                def low_probabilities(a):
                    for qt in range(NT):
                        ve.wait_ge(S["mla_pt_hi"], hp * 8 + (4 * a + qt + 1))
                        c, m = 128 * (qt * (qt + 1) // 2), 128 * (qt + 1)
                        lo(PKL[:, c:c + m], B[4 + qt][:, 0:m], PKH[:, c:c + m]).then_inc(S["mla_pt_split"], 1)
                        ve.drain().then_inc(free[4 + qt], 1)

                def twice_silu(a):
                    ve.wait_ge(S["mla_tanh"], hp * 2 + (a + 1))
                    v.scalar_tensor_tensor(MU[:, a, :], TG[:, a, :], 1.0, B[a][:, :], ALU.add, ALU.mult).then_inc(free[a], 1)
                    ve.drain()

                def gated(a):
                    ve.wait_ge(S["mla_o_made"], hp * 2 + (a + 1))
                    v.scalar_tensor_tensor(SQ[:, a, :], B[2 + a][:, :], 0.5, MU[:, a, :], ALU.mult, ALU.mult)\
                        .then_inc(S["mla_y_f32"], 1)
                    ve.drain().then_inc(free[2 + a], 1)

                def low_y(a):
                    ve.wait_ge(S["mla_y_hi"], hp * 2 + (a + 1))
                    lo(MYL[:, a, :], SQ[:, a, :], MYH[:, a, :]).then_inc(S["mla_y_split"], 1)

                maxima(0)
                probabilities(0)
                twice_silu(0)
                low_probabilities(0)
                maxima(1)
                probabilities(1)
                gated(0)
                low_y(0)
                twice_silu(1)
                low_probabilities(1)
                gated(1)
                low_y(1)
                for f in range(KD):
                    tile_done(ve, "mla_out_made", f, KD, hp * 4 + (N_MLA + 3), hp * 7)
                    v.tensor_tensor(ACC[:, f, :], ACC[:, f, :], B[f % 4][:, :], ALU.add).then_inc(free[f % 4], 1)

            per_layer_input(1)
            norm("mix0")

            mean, root, inv = ST[:, 2, :], ST[:, 5, :], ST[:, 3, :]
            ve.wait_ge(S["ws_loaded"], 32)
            v.tensor_tensor(WT[:, :, :], WT[:, :, :], UPPER.unsqueeze(1).to_broadcast([128, GROUPS, 128]), ALU.mult)\
                .then_inc(S["wt_masked"], 1)
            ve.wait_ge(S["mix_gelu"], 8)
            v.tensor_tensor(mean, ST[:, 0, :], ST[:, 1, :], ALU.add)
            ve.drain()
            v.tensor_scalar(mean, mean, 1.0 / 1024, None, ALU.mult)
            ve.drain()
            for tt in range(NT):
                v.tensor_scalar(NV[:, tt, :], NV[:, tt, :], mean[:, tt:tt + 1], None, ALU.subtract)\
                    .then_inc(S["nv_centred"], 1)
            ve.wait_ge(S["nv_root"], 1)
            v.reciprocal(inv, root)
            ve.drain()
            for tt in range(NT):
                v.tensor_scalar(NV[:, tt, :], NV[:, tt, :], inv[:, tt:tt + 1], None, ALU.mult).then_inc(S["mix_f32"], 1)
            for tt in range(NT):
                ve.wait_ge(S["mix_hi"], tt + 1)
                lo(NVL[:, tt, :], NV[:, tt, :], NVH[:, tt, :]).then_inc(S["mix_split"], 1)
            ve.wait_ge(S["wt_hi"], 1)
            lo(WTL[:, :, :], WT[:, :, :], WTH[:, :, :]).then_inc(S["wt_split"], 1)
            for j in range(2):
                ve.wait_ge(S["rowsum_made"], j + 1)
                for g in range(4 * j, 4 * j + 4):
                    end = v.scalar_tensor_tensor(BT[:, g, :], B[4 + j][:, 128 * (g % 4):128 * (g % 4) + 128], gain("lnb", g),
                                                 BS[:, g, :], ALU.mult, ALU.add)
                end.then_inc(free[4 + j], 1)
            ve.wait_ge(S["mix_u"], 1)

            def tokens(t):
                return t.rearrange("p (t n) -> p t n", t=NT)

            for g in range(GROUPS + 1):
                if g < GROUPS:
                    ve.drain()
                    ve.wait_ge(S["mixed"], g + 1)
                    v.scalar_tensor_tensor(tokens(T[:, g % 2, :]), tokens(B[g % 4][:, :]), gain("lng", g),
                                           BT[:, g, :].unsqueeze(1).to_broadcast([128, NT, 128]), ALU.mult, ALU.add)\
                        .then_inc(free[g % 4], 1)
                    ve.drain()
                    v.tensor_tensor(T[:, g % 2, :], T[:, g % 2, :], GU[:, g, :], ALU.mult).then_inc(S["mix_f32"], 1)
                if g > 0:
                    ve.wait_ge(S["mix_hi"], NT + g)
                    gs = slice(128 * (g - 1), 128 * g)
                    lo(NVL[:, :, gs], tokens(T[:, (g - 1) % 2, :]), NVH[:, :, gs]).then_inc(S["mix_split"], 1)
            for f in range(KD):
                tile_done(ve, "mix_out_made", f, 2, N_MIX + 8 + f // 2)
                v.tensor_tensor(X[:, f, :], X[:, f, :], B[f % 4][:, :], ALU.add).then_inc(S["mix_done"], 1)
                ve.drain().then_inc(free[f % 4], 1)

            def mlp(L, n0):
                at = 4 * CHUNKS * L

                def chunk(c, last):
                    for j in range(2):
                        for f in range(2 * j, 2 * j + 2):
                            ve.drain()
                            ve.wait_ge(S["mlp_relu"], c * 4 + (at + f + 1))
                            v.tensor_tensor(T[:, f, :], TG[:, f % 2, :], TG[:, f % 2, :], ALU.mult)\
                                .then_inc(S["mlp_hid_f32"], 1)
                        for f in range(2 * j, 2 * j + 2):
                            ve.wait_ge(S["mlp_hid_hi"], c * 4 + (at + f + 1))
                            lo(HIDL[:, f, :], T[:, f, :], HIDH[:, f, :]).then_inc(S["mlp_hid_split"], 1)
                    for f in range(KD):
                        b = 4 + f if f < 4 else f - 4
                        tile_done(ve, "mlp_down_made", f, 4, c * 4 + (n0 + 2 + f // 4), c * 6, 6 * CHUNKS * L)
                        end = v.tensor_tensor(X[:, f, :], X[:, f, :], B[b][:, :], ALU.add)
                        if last:
                            end.then_inc(S["mlp_done"], 1)
                            ve.drain().then_inc(free[b], 1)
                        else:
                            end.then_inc(free[b], 1)

                with ve.Fori(0, CHUNKS - 1) as c:
                    chunk(c, False)
                chunk(CHUNKS - 1, True)

            norm("mlp0")
            mlp(0, N_MLP0)

            norm("mix1")
            ve.wait_ge(S["tab_loaded"], 64)
            for half in range(2):
                for g in range(3):
                    u = 3 * half + g
                    for f in range(4):
                        ve.wait_ge(S["dil_qk_hi"], 4 * u + f + 1)
                        dh, dl = ((DQH, DQL) if f < 2 else (DKH, DKL))
                        lo(in_order(dl[:, f % 2, :], g), natural(B[f], g), in_order(dh[:, f % 2, :], g))\
                            .then_inc(S["dil_qk_split"], 1)
                        ve.drain().then_inc(free[f], 1)
                    for j in range(2):
                        ve.wait_ge(S["dil_v_hi"], 2 * u + j + 1)
                        vj = slice(2 * j, 2 * j + 2)
                        lo(DVL[:, vj, :].rearrange("p t n -> p (t n)"), B[j][:, :],
                           DVH[:, vj, :].rearrange("p t n -> p (t n)")).then_inc(S["dil_v_split"], 1)
                        ve.drain().then_inc(free[j], 1)
                    for hh in range(4):
                        a, head = 4 * u + hh, 4 * half + hh
                        mx, sm = MXS[:, g, hh, :], SUMS[:, g, hh, :]
                        cur = T[:, 0, :].rearrange("p (t n) -> p t n", t=NT)
                        prev = T[:, 1, 0:384].rearrange("p (t n) -> p t n", t=NT - 1)

                        def logits(dst, b, m, kind):
                            v.scalar_tensor_tensor(dst, B[b][:, 0:128 * m].rearrange("p (t n) -> p t n", t=m), HEAD_DIM ** -0.5,
                                                   TAB[:, kind, head, :].unsqueeze(1).to_broadcast([128, m, 128]),
                                                   ALU.mult, ALU.add).then_inc(free[b], 1)

                        ve.wait_ge(S["dil_s_made"], a + 1)
                        logits(cur, 4, NT, g)
                        if g == 0:
                            logits(prev, 5, NT - 1, 3)
                        ve.drain()
                        v.reduce_max(mx, cur, AX.X)
                        if g == 0:
                            v.reduce_max(ST[:, 6, 0:3], prev, AX.X)
                            ve.drain()
                            v.tensor_tensor(mx[:, 1:4], mx[:, 1:4], ST[:, 6, 0:3], ALU.max)
                        ve.drain()
                        v.tensor_tensor(cur, cur, mx.unsqueeze(2).to_broadcast([128, NT, 128]), ALU.subtract)
                        if g == 0:
                            v.tensor_tensor(prev, prev, mx[:, 1:4].unsqueeze(2).to_broadcast([128, NT - 1, 128]), ALU.subtract)
                        ve.drain().then_inc(S["dil_centred"], 1)
                        ve.wait_ge(S["dil_exp"], a + 1)
                        v.reduce_sum(sm, cur, AX.X)
                        if g == 0:
                            v.reduce_sum(ST[:, 6, 0:3], prev, AX.X)
                            ve.drain()
                            v.tensor_tensor(sm[:, 1:4], sm[:, 1:4], ST[:, 6, 0:3], ALU.add)
                        ve.drain()
                        v.reciprocal(ST[:, 7, :], sm)
                        ve.drain()
                        v.tensor_tensor(cur, cur, ST[:, 7, :].unsqueeze(2).to_broadcast([128, NT, 128]), ALU.mult)
                        if g == 0:
                            v.tensor_tensor(prev, prev, ST[:, 7, 1:4].unsqueeze(2).to_broadcast([128, NT - 1, 128]), ALU.mult)
                        ve.drain().then_inc(S["dil_p_ready"], 1)
                        ve.wait_ge(S["dil_pt_hi"], a + 1)
                        lo(DPL[:, 0, :], B[6][:, :], DPH[:, 0, :]).then_inc(free[6], 1)
                        if g == 0:
                            lo(DPL[:, 1, 0:384], B[7][:, 0:384], DPH[:, 1, 0:384]).then_inc(free[7], 1)
                        ve.drain().then_inc(S["dil_pt_split"], 1)
                ve.drain().then_inc(S["dil_sums"], 1)
                ve.wait_ge(S["dil_ln"], half + 1)
                flat = [t[:, :, :, :].rearrange("p a b c -> p (a b c)") for t in (SUMS, MXS)]
                v.tensor_tensor(flat[0], flat[0], flat[1], ALU.add)
                for pr in range(2):
                    w = 2 * half + pr
                    ve.drain()
                    for g in range(3):
                        if pr > 0 and g == 0:
                            ve.wait_ge(S["dil_lse_made"], 3 * w)
                        for e in range(2):
                            dst = LSE_COLS[g].rearrange("p (t e n) -> p e t n", t=NT, e=2)[:, e]
                            end = v.tensor_copy(dst, SUMS[:, g, 2 * pr + e, :].unsqueeze(2).to_broadcast([128, NT, 64]))
                        end.then_inc(S["dil_lse"], 1)
                    ve.wait_ge(S["dil_lse_copied"], w + 1)
                    L3, top = [LSE[:, g, :] for g in range(3)], TOP
                    v.tensor_tensor(top, L3[0], L3[1], ALU.max)
                    ve.drain()
                    v.tensor_tensor(top, top, L3[2], ALU.max)
                    ve.drain()
                    for g in range(3):
                        v.tensor_tensor(L3[g], L3[g], top, ALU.subtract)
                    ve.drain().then_inc(S["dil_lse_centred"], 1)
                    ve.wait_ge(S["dil_weights"], w + 1)
                    v.tensor_tensor(top, L3[0], L3[1], ALU.add)
                    for g in range(3):
                        v.tensor_tensor(OG[pr][:, g, :], OG[pr][:, g, :], L3[g], ALU.mult)
                    ve.drain()
                    v.tensor_tensor(top, top, L3[2], ALU.add)
                    v.tensor_tensor(OG[pr][:, 0, :], OG[pr][:, 0, :], OG[pr][:, 1, :], ALU.add)
                    ve.drain()
                    v.reciprocal(top, top)
                    v.tensor_tensor(OG[pr][:, 0, :], OG[pr][:, 0, :], OG[pr][:, 2, :], ALU.add)
                    ve.drain()
                    v.tensor_tensor(DY, OG[pr][:, 0, :], top, ALU.mult).then_inc(S["dil_y_f32"], 1)
                    ve.wait_ge(S["dil_y_hi"], w + 1)
                    lo(DYL[:, w, :], DY, DYH[:, w, :]).then_inc(S["dil_y_split"], 1)
            for f in range(KD):
                tile_done(ve, "dil_out_made", f, 4, N_DILOUT + f // 4)
                v.tensor_tensor(X[:, f, :], X[:, f, :], B[f % 4][:, :], ALU.add).then_inc(S["dil_done"], 1)
                ve.drain().then_inc(free[f % 4], 1)

            norm("mlp1")
            mlp(1, N_MLP1)

            add_squares("final", KD)
            inverse_root("final")
            for k in range(KD):
                v.scalar_tensor_tensor(ACC[:, k, :], X[:, k, :], gain("final", k), R[:, :], ALU.mult, ALU.mult)\
                    .then_inc(S["final_ready"], 1)


def _bucket(distance):
    d = np.asarray(distance)
    large = 16 + (np.log(np.maximum(d, 1).astype(np.float32) / np.float32(16)) / np.float32(np.log(2048 / 16)) * 16).astype(np.int32)
    return np.where(d < 16, d, np.minimum(large, 31))


def _constants():
    c = np.zeros((128, 3 * 128 + 8), np.float32)
    p = np.arange(128)
    c[:, 0:128] = np.eye(128)
    c[:, 128:256] = np.where(p[None, :] <= p[:, None], 0.0, NEG)
    c[:, 256:384] = p[:, None] <= p[None, :]
    c[:, 384] = (10000.0 ** (-p / 128.0)).astype(np.float32)
    c[:, 385] = (10000.0 ** (-(p % 32) / 32.0)).astype(np.float32)
    c[:, 386] = np.where((p % 64) < 32, -1.0, 1.0)
    log_g = np.log(1.0 - 2.0 ** (-5.0 - np.arange(RET_HEADS)))
    rel = np.arange(512)[None, :] - p[:, None]
    decay = np.where(rel[None] >= 0, np.exp(np.maximum(rel, 0)[None] * log_g[:, None, None]), 0.0) * RET_QK ** -0.5
    onehot = np.zeros((33, 4, 256), np.float32)
    y = np.arange(256)
    for kind, (dist, ok) in enumerate((
        (127 - y, y <= 127),
        (4 * (127 - y), y <= 127),
        (4 * (127 - y), (y <= 127) & ((127 - y) % 4 == 0)),
        (255 - y, y >= 127),
    )):
        b = np.where(ok, _bucket(np.where(ok, dist, 0)), 32)
        onehot[b, kind, y] = 1.0
    return c, decay.astype(np.float32), onehot.reshape(33, 1024)


def _blocks(w, rows, cols):
    w = w[rows][:, cols]
    return w.reshape(-1, 128, w.shape[1]).transpose(1, 0, 2).reshape(128, -1)


def _lay_out_panels(a):
    out = np.empty((NPANEL, 128, PANEL), np.float32)
    at = [0]
    every = slice(None)

    def put(*parts):
        out[at[0]] = np.concatenate(parts, axis=1)
        at[0] += 1

    def cols(start, n=256):
        return slice(start, start + n)

    w, wo = a["ret_w_in"][0], a["ret_w_out"][0]
    for h in range(RET_HEADS):
        put(_blocks(w, every, cols(256 * h)))
        put(_blocks(w, every, cols(1024 + 256 * h)))
        for j in range(2):
            put(_blocks(w, cols(512 * j, 512), cols(2048 + 512 * h, 512)))
        for j in range(2):
            put(_blocks(w, every, cols(4096 + 512 * h + 256 * j)))
        for j in range(2):
            put(_blocks(wo, cols(512 * h, 512), cols(512 * j, 512)))

    def per_layer_input(L):
        put(_blocks(a["ple_w_proj"][L], every, every))
        for j in range(4):
            put(_blocks(a["ple_w_gate"][L], every, cols(256 * j)))

    per_layer_input(0)
    w = a["mla_w_in"][0]
    for j in range(4):
        put(_blocks(w, every, cols(256 * j)))
    half = np.arange(32)
    straight = np.concatenate([half, half + 32])
    swapped = np.concatenate([half + 32, half])
    put(_blocks(w, every, 1024 + np.concatenate([straight, straight, swapped, swapped])))
    uq, uk, uv, wo = a["mla_w_uq"][0], a["mla_w_uk"][0], a["mla_w_uv"][0], a["mla_w_out"][0]
    uk, uv = uk.reshape(KV_LORA, -1), uv.reshape(KV_LORA, -1)
    for hp in range(PAIRS):
        qa, qb = 192 * 2 * hp, 192 * (2 * hp + 1)
        nope = np.concatenate([np.arange(qa, qa + 128), np.arange(qb, qb + 128)])
        rope = np.concatenate([q + 128 + o for o in (straight, swapped) for q in (qa, qb)])
        put(_blocks(uq, every, nope), _blocks(uk, every, cols(256 * hp)))
        put(_blocks(uq, every, rope), _blocks(uv, every, cols(256 * hp)))
        put(_blocks(w, every, cols(1088 + 256 * hp)))
        put(_blocks(wo, cols(256 * hp), every))
    per_layer_input(1)
    w, wo = a["a_w_in_2"][0], a["a_w_out_2"][0]
    for cc in range(2):
        for j in range(2):
            put(_blocks(w, cols(512 * j, 512), cols(1024 + 512 * cc, 512)))
    for j in range(4):
        put(_blocks(w, every, cols(256 * j)))
    for j in range(4):
        put(_blocks(wo, every, cols(256 * j)))

    def mlp(L):
        up, down = a["w_up_2"][L], a["w_down_2"][L]
        for c in range(CHUNKS):
            for j in range(2):
                put(_blocks(up, every, cols(HID * c + 256 * j)))
            for j in range(2):
                put(_blocks(down, cols(HID * c, HID), cols(512 * j, 512)))

    mlp(0)
    w, wo = a["b_w_qkv_2"][0], a["b_w_out_2"][0]
    for half_ in range(2):
        for g in range(3):
            for j in range(3):
                put(_blocks(w, every, cols(1536 * j + 512 * g + 256 * half_)))
    for j in range(2):
        put(_blocks(wo, every, cols(512 * j, 512)))
    mlp(1)
    assert at[0] == NPANEL
    return out


def _tiles(v):
    return v.reshape(-1, 128).T


def kernel(**inputs):
    import concourse.bacc as bacc
    from concourse.bass_utils import run_bass_kernel_spmd

    a = {k: np.asarray(v) for k, v in inputs.items()}
    consts, decay, onehot = _constants()
    gains = [a["pre_norm_g"][0], a["post_norm_g"][0], a["pre_norm_g"][1], a["post_norm_g"][1], a["mix_norm_g_2"][0],
             a["mlp_norm_g_2"][0], a["mix_norm_g_2"][1], a["mlp_norm_g_2"][1], a["final_norm_g_2"],
             a["mla_q_norm_g"][0], a["mla_kv_norm_g"][0], a["a_ln_g_2"][0], a["a_ln_b_2"][0]]
    arrays = {
        "panels": _lay_out_panels(a),
        "gains": np.concatenate([_tiles(g) for g in gains], axis=1),
        "xin": a["x"][0].T.reshape(KD, 128, SEQ),
        "pin": a["p"][:, 0].transpose(0, 2, 1).reshape(2, 2, 128, SEQ),
        "pos": np.broadcast_to(a["positions"].astype(np.int32), (128, SEQ)),
        "gn": a["ret_gn_g"][0].reshape(RET_HEADS, 4, 128).transpose(0, 2, 1),
        "decay": decay,
        "consts": consts,
        "rel": a["rel_bias_2"],
        "onehot": onehot,
        "wsT": a["a_w_s_2"][0].transpose(2, 0, 1),
        "bs": np.broadcast_to(a["a_b_s_2"][0], (128, GROUPS, 128)),
    }
    arrays = {k: np.ascontiguousarray(v) for k, v in arrays.items()}
    nc = bacc.Bacc("TRN2", target_bir_lowering=False, num_devices=1)
    args = {k: nc.dram_tensor(k, v.shape, mybir.dt.from_np(v.dtype), kind="ExternalInput").ap() for k, v in arrays.items()}
    out = nc.dram_tensor("out", (KD, 128, SEQ), mybir.dt.float32, kind="ExternalOutput").ap()
    scratch = nc.dram_tensor("scratch", (4, 8, 128, 256), mybir.dt.float32, kind="Internal").ap()
    xsave = nc.dram_tensor("xsave", (KD, 128, SEQ), mybir.dt.float32, kind="Internal").ap()
    program(nc, out=out, scratch=scratch, xsave=xsave, **args)
    r = run_bass_kernel_spmd(nc, [arrays], core_ids=[0])
    return r.results[0]["out"].reshape(D_MODEL, SEQ).T[None]
```

```python
from contextlib import ExitStack

import numpy as np

import concourse.bass as bass
from concourse import mybir

D_MODEL, SEQ = 1024, 512
KD = D_MODEL // 128
NT = SEQ // 128
RET_HEADS, RET_QK, RET_V = 4, 256, 512
MLA_HEADS, NOPE, ROPE, MLA_V = 16, 128, 64, 128
Q_LORA, KV_LORA = 768, 256
KQ, KC = Q_LORA // 128, KV_LORA // 128
PAIRS = MLA_HEADS // 2
GROUPS = 8
D_FF = 4096
HID = 512
CHUNKS = D_FF // HID
DILATIONS = (1, 4, 16)
HEAD_DIM = 64
EPS = 1e-6
NEG = -1e30
PANEL = 2048

N_RET = 0
N_PLE0 = N_RET + 8 * RET_HEADS
N_MLAIN = N_PLE0 + 5
N_MLA = N_MLAIN + 5
N_PLE1 = N_MLA + 4 * PAIRS
N_MIX = N_PLE1 + 5
N_MLP0 = N_MIX + 12
N_DIL = N_MLP0 + 4 * CHUNKS
N_DILOUT = N_DIL + 18
N_MLP1 = N_DILOUT + 2
NPANEL = N_MLP1 + 4 * CHUNKS

GAINS = (("pre0", 8), ("post0", 8), ("pre1", 8), ("post1", 8), ("mix0", 8), ("mlp0", 8), ("mix1", 8),
         ("mlp1", 8), ("final", 8), ("qn", KQ), ("kvn", KC), ("lng", GROUPS), ("lnb", GROUPS))
GAIN_AT, _at = {}, 0
for _name, _n in GAINS:
    GAIN_AT[_name] = _at
    _at += _n
NGAIN = _at

def _parts(value, bits, n):
    out, rest = [], value
    for _ in range(n):
        e = np.floor(np.log2(rest))
        q = 2.0 ** (e - bits + 1)
        part = np.floor(rest / q) * q
        out.append(float(part))
        rest -= part
    return out


TWO_PI = 2.0 * np.pi
COARSE = 2.0 ** 15


class Signals(dict):

    def __init__(self, make):
        super().__init__()
        self.make = make

    def __missing__(self, name):
        self[name] = self.make(name)
        return self[name]


NORMS = ("pre0", "post0", "pre1", "cq", "ckv", "post1", "mix0", "mlp0", "mix1", "mlp1", "final")
FULL = tuple(n for n in NORMS if n not in ("cq", "ckv"))
SPLIT = ("pre0", "pre1", "mix0", "mlp0", "mix1", "mlp1")


class BankUses:
    GIVEN = (0, 1, 2, 3, 7)

    def __init__(self):
        self.n = [int(b in self.GIVEN) for b in range(8)]
        self.i, self.per = None, None

    def loop(self, i, per):
        self.i, self.per, self.start = i, per, list(self.n)

    def end(self, trips):
        assert [a - b for a, b in zip(self.n, self.start)] == list(self.per), (self.n, self.start)
        self.n = [s + trips * p for s, p in zip(self.start, self.per)]
        self.i = None

    def take(self, b):
        v = self.n[b]
        self.n[b] += 1
        if self.i is None:
            return v
        return v + self.i * self.per[b]


def program(nc, panels, gains, xin, pin, pos, gn, decay, consts, rel, onehot, wsT, bs, out, scratch, xsave):
    f32, f32r = mybir.dt.float32, mybir.dt.float32r
    ALU, ACT, AX = mybir.AluOpType, mybir.ActivationFunctionType, mybir.AxisListType
    i32 = mybir.dt.int32
    MLA_SCALE = float(NOPE + ROPE) ** -0.5
    ctx = ExitStack()
    with ctx:
        def sb(name, shape, dt=f32, c=ctx):
            return c.enter_context(nc.sbuf_tensor(name, shape, dt))

        S = Signals(lambda name: ctx.enter_context(nc.semaphore(name)))
        B = [ctx.enter_context(nc.psum_tensor(f"bank{b}", [128, 512], f32)) for b in range(8)]
        free = [S[f"bank{b}_free"] for b in range(8)]

        RAW = sb("RAW", [128, 2, PANEL])
        WH = sb("WH", [128, 2, PANEL], f32r)
        WL = sb("WL", [128, 2, PANEL], f32r)
        HH = sb("HH", [128, KD, 512], f32r)
        HL = sb("HL", [128, KD, 512], f32r)
        ACC = sb("ACC", [128, KD, 512])
        G = sb("G", [128, NGAIN])
        CONST = sb("CONST", [128, 3 * 128 + 8])
        IDENT, CAUSAL, UPPER = (CONST[:, 128 * j:128 * j + 128] for j in range(3))
        FREQ1, FREQ2, SIGN = (CONST[:, 384 + j:385 + j] for j in range(3))
        ONES = sb("ONES", [128, 128])
        EPSC = sb("EPSC", [128, 2])
        R = sb("R", [128, 512])
        SS = sb("SS", [128, 512])
        SQ = sb("SQ", [128, 2, 512])
        T = sb("T", [128, 4, 512])
        TG = sb("TG", [128, 2, 512])
        ST = sb("ST", [128, 8, 4])

        with ExitStack() as c:
            CQH, CQL = sb("CQH", [128, KQ, 512], f32r, c), sb("CQL", [128, KQ, 512], f32r, c)
            CKH, CKL = sb("CKH", [128, KC, 512], f32r, c), sb("CKL", [128, KC, 512], f32r, c)
            KRH, KRL = sb("KRH", [128, 512], f32r, c), sb("KRL", [128, 512], f32r, c)
            MQH, MQL = sb("MQH", [128, 4, 512], f32r, c), sb("MQL", [128, 4, 512], f32r, c)
            QRH, QRL = sb("QRH", [128, 512], f32r, c), sb("QRL", [128, 512], f32r, c)
            MVH, MVL = sb("MVH", [128, NT, 256], f32r, c), sb("MVL", [128, NT, 256], f32r, c)
            PKH, PKL = sb("PKH", [128, 1280], f32r, c), sb("PKL", [128, 1280], f32r, c)
            COS2, SIN2 = sb("COS2", [128, 512], f32, c), sb("SIN2", [128, 512], f32, c)
            MU = sb("MU", [128, 2, 512], f32, c)
        MYH, MYL = MQH, MQL
        X = sb("X", [128, KD, 512])
        with ExitStack() as c:
            QH, QL = sb("QH", [128, 2, 512], f32r, c), sb("QL", [128, 2, 512], f32r, c)
            KH, KL = sb("KH", [128, 2, 512], f32r, c), sb("KL", [128, 2, 512], f32r, c)
            VH, VL = sb("VH", [128, NT, 512], f32r, c), sb("VL", [128, NT, 512], f32r, c)
            AH, AL = sb("AH", [128, 4, 512], f32r, c), sb("AL", [128, 4, 512], f32r, c)
            YH, YL = AH, AL
            U = sb("U", [128, 4, 512], f32, c)
            O = sb("O", [128, 4, 512], f32, c)
            COS1, SIN1 = sb("COS1", [128, 512], f32, c), sb("SIN1", [128, 512], f32, c)
            DEC = sb("DEC", [128, 512], f32, c)
            GN = sb("GN", [128, 4], f32, c)
        with ExitStack() as c:
            PJ = sb("PJ", [128, KD, 512], f32, c)
            PF = sb("PF", [128, 2, 512], f32, c)
            PH, PL = sb("PH", [128, 2, 512], f32r, c), sb("PL", [128, 2, 512], f32r, c)
        with ExitStack() as c:
            HIDH, HIDL = sb("HIDH", [128, 4, 512], f32r, c), sb("HIDL", [128, 4, 512], f32r, c)
        with ExitStack() as c:
            NVH, NVL = sb("NVH", [128, NT, 1024], f32r, c), sb("NVL", [128, NT, 1024], f32r, c)
            WTH, WTL = sb("WTH", [128, GROUPS, 128], f32r, c), sb("WTL", [128, GROUPS, 128], f32r, c)
            WT = sb("WT", [128, GROUPS, 128], f32, c)
            BT = sb("BT", [128, GROUPS, 128], f32, c)
            BS = sb("BS", [128, GROUPS, 128], f32, c)
            GU = sb("GU", [128, GROUPS, 512], f32, c)
        NV = ACC[:, :, :].rearrange("p k n -> p (k n)").rearrange("p (t n) -> p t n", t=NT)
        with ExitStack() as c:
            DQH, DQL = sb("DQH", [128, 2, 512], f32r, c), sb("DQL", [128, 2, 512], f32r, c)
            DKH, DKL = sb("DKH", [128, 2, 512], f32r, c), sb("DKL", [128, 2, 512], f32r, c)
            DVH, DVL = sb("DVH", [128, NT, 256], f32r, c), sb("DVL", [128, NT, 256], f32r, c)
            DPH, DPL = sb("DPH", [128, 2, 512], f32r, c), sb("DPL", [128, 2, 512], f32r, c)
            DYH, DYL = sb("DYH", [128, 4, 512], f32r, c), sb("DYL", [128, 4, 512], f32r, c)
            TAB = sb("TAB", [128, 4, 8, 128], f32, c)
            OG1 = sb("OG1", [128, 3, 512], f32, c)
            MXS = sb("MXS", [128, 3, 4, 4], f32, c)
            SUMS = sb("SUMS", [128, 3, 4, 4], f32, c)
        OG = [ACC[:, 0:3, :], OG1[:, :, :]]
        LSE_COLS = [TG[:, 0, :], TG[:, 1, :], T[:, 2, :]]
        LSE, TOP, DY = ACC[:, 3:6, :], T[:, 3, :], SQ[:, 0, :]
        REL = ST[0:33, :, :].rearrange("p a b -> p (a b)")[:, 0:24]
        ONEHOT = TG[0:33, :, :]
        ROWS = ACC[0:24, 0:2, :]
        ROWS8 = [ACC[8 * g:8 * g + 8, 0:2, :] for g in range(3)]

        def in_order(t, g):
            return t[:, :].rearrange("p (r a) -> p r a", r=4)

        def natural(t, g):
            return t[:, :].rearrange("p (r a) -> p r a", r=4) if g == 0 else t[:, :].rearrange("p (a r) -> p r a", r=4)

        def tile_done(e, sig, f, per, n, before=0, base=0):
            if f % per == per - 1:
                e.wait_ge(panel_used, n + 1)
            else:
                e.wait_ge(S[sig], before + (base + (f // per) * (per - 1) + f % per + 1))

        raw_loaded = (S["raw_even_loaded"], S["raw_odd_loaded"])
        hi_ready, lo_ready, panel_used = S["panel_hi_ready"], S["panel_lo_ready"], S["panel_used"]

        block = ctx.enter_context(nc.Block())

        @block.sync
        def _(sp):
            def load(m, slot):
                sp.dma_start(RAW[:, slot, :], panels[m]).then_inc(raw_loaded[slot], 16)

            load(0, 0)
            load(1, 1)
            with sp.Fori(0, (NPANEL - 3) // 2) as i:
                for s in (0, 1):
                    m = sp.snap(i * 2 + (2 + s))
                    sp.wait_ge(lo_ready, i * 2 + (1 + s))
                    sp.dma_start(RAW[:, s, :], panels[bass.ds(m, 1)].rearrange("a p c -> (a p) c"))\
                      .then_inc(raw_loaded[s], 16)
            sp.wait_ge(lo_ready, NPANEL - 2)
            load(NPANEL - 1, (NPANEL - 1) % 2)
            for k in range(KD):
                sp.wait_ge(S["final_ready"], k + 1)
                sp.dma_start(out[k], ACC[:, k, :]).then_inc(S["out_stored"], 16)
            sp.wait_ge(S["out_stored"], 16 * KD)

        @block.gpsimd
        def _(gp):
            def low(s):
                return gp.tensor_tensor(WL[:, s, :], RAW[:, s, :], WH[:, s, :].bitcast(f32), ALU.subtract)

            for m in (0, 1):
                gp.wait_ge(hi_ready, m + 1)
                low(m).then_inc(lo_ready, 1)
            with gp.Fori(0, (NPANEL - 3) // 2) as i:
                for s in (0, 1):
                    gp.wait_ge(hi_ready, i * 2 + (3 + s))
                    gp.wait_ge(panel_used, i * 2 + (1 + s))
                    low(s).then_inc(lo_ready, 1)
            gp.wait_ge(hi_ready, NPANEL)
            gp.wait_ge(panel_used, NPANEL - 2)
            low((NPANEL - 1) % 2).then_inc(lo_ready, 1)

        @block.tensor
        def _(pe):
            uses = BankUses()

            def bank(b):
                v = uses.take(b)
                if not isinstance(v, int) or v > 0:
                    pe.wait_ge(free[b], v)
                return B[b]

            def panel(n, slot):
                pe.wait_ge(lo_ready, n + 1)
                return WH[:, slot, :], WL[:, slot, :]

            def signal(end, sig, last):
                end.then_inc(panel_used if last else S[sig], 1)

            def mm3(o, ah, al, bh, bl, start, stop):
                nc.tensor.matmul(o, ah, bh, start=start, stop=False)
                nc.tensor.matmul(o, ah, bl, start=False, stop=False)
                return nc.tensor.matmul(o, al, bh, start=False, stop=stop)

            def tile_of(o, w, f, width, xh, xl, k0, k1, first=True, last=True, at=0, wait=None):
                wh, wl = w
                for k in range(k0, k1):
                    if wait is not None:
                        wait(k)
                    c = at + (k - k0) * width + f * 128
                    end = mm3(o, wh[:, c:c + 128], wl[:, c:c + 128], xh[:, k, :], xl[:, k, :],
                              first and k == k0, last and k == k1 - 1)
                return end

            def tiles_together(os, w, width, xh, xl, nk, wait, f0=0):
                wh, wl = w
                ends = [None] * len(os)
                for k in range(nk):
                    wait(k)
                    for i, o in enumerate(os):
                        c = k * width + (f0 + i) * 128
                        ends[i] = mm3(o[:, :], wh[:, c:c + 128], wl[:, c:c + 128], xh[:, k, :], xl[:, k, :],
                                      k == 0, k == nk - 1)
                return ends

            def sum_of_squares(name, squares=SS[:, :]):
                o = bank(4)
                pe.wait_ge(S["norm_squares"], NORMS.index(name) + 1)
                nc.tensor.matmul(o[:, :], ONES[:, :], squares, start=True, stop=True).then_inc(S["norm_sum"], 1)

            def of_h(name):
                return lambda k: pe.wait_ge(S["norm_h_split"], KD * SPLIT.index(name) + k + 1)

            pe.wait_ge(S["rel_loaded"], 32)
            pe.wait_ge(S["rel_neg"], 1)
            for j in (0, 1):
                nc.tensor.matmul(bank(5 + j)[0:24, :], REL, ONEHOT[:, j, :], start=True, stop=True)\
                  .then_inc(S["bias_rows"], 1)
            sum_of_squares("pre0")

            with pe.Fori(0, RET_HEADS) as h:
                uses.loop(h, [5] * 4 + [3, 2, 2, 2])
                n = h * 8
                wait_h = of_h("pre0")
                w = panel(n, 0)
                tiles_together([bank(0), bank(1)], w, 256, HH, HL, KD, wait_h)[1].then_inc(panel_used, 1)
                w = panel(n + 1, 1)
                for f in range(2):
                    end = tile_of(bank(2 + f)[:, :], w, f, 256, HH, HL, 0, KD)
                end.then_inc(panel_used, 1)
                os_ = [bank(tt) for tt in range(NT)]
                for j in range(2):
                    wh, wl = panel(n + 2 + j, j % 2)
                    for tt in range(NT):
                        ts = slice(128 * tt, 128 * tt + 128)
                        for k in range(4):
                            end = mm3(os_[tt][:, :], HH[:, 4 * j + k, ts], HL[:, 4 * j + k, ts],
                                      wh[:, 512 * k:512 * k + 512], wl[:, 512 * k:512 * k + 512],
                                      j == 0 and k == 0, j == 1 and k == 3)
                        if j == 1 or tt == NT - 1:
                            signal(end, "ret_v_made", tt == NT - 1)
                pe.wait_ge(S["ret_qk_split"], h * 4 + 4)
                for jt in range(NT):
                    o = bank(4 + jt)
                    for dk in range(2):
                        ks, qs = slice(128 * jt, 128 * jt + 128), slice(128 * jt, 512)
                        end = mm3(o[:, 0:512 - 128 * jt], KH[:, dk, ks], KL[:, dk, ks], QH[:, dk, qs], QL[:, dk, qs],
                                  dk == 0, dk == 1)
                    end.then_inc(S["ret_a_made"], 1)
                w = panel(n + 4, 0)
                for f in range(2):
                    end = tile_of(bank(f)[:, :], w, f, 256, HH, HL, 0, KD)
                    signal(end, "ret_g_made", f == 1)
                pe.wait_ge(S["ret_v_split"], h * 4 + 4)
                for vt in range(4):
                    o = bank(4 + vt)
                    vs = slice(128 * vt, 128 * vt + 128)
                    for jt in range(NT):
                        if vt == 0:
                            pe.wait_ge(S["ret_a_split"], h * 4 + (jt + 1))
                        m = 512 - 128 * jt
                        end = mm3(o[:, 128 * jt:512], VH[:, jt, vs], VL[:, jt, vs], AH[:, jt, 0:m], AL[:, jt, 0:m],
                                  jt == 0, jt == NT - 1)
                    end.then_inc(S["ret_o_made"], 1)
                w = panel(n + 5, 1)
                end = tile_of(bank(2)[:, :], w, 0, 256, HH, HL, 0, KD)
                end.then_inc(S["ret_g_made"], 1)
                o = bank(4)
                pe.wait_ge(S["ret_squares"], h + 1)
                nc.tensor.matmul(o[:, :], ONES[:, :], SS[:, :], start=True, stop=True).then_inc(S["ret_sum"], 1)
                end = tile_of(bank(3)[:, :], w, 1, 256, HH, HL, 0, KD)
                end.then_inc(panel_used, 1)
                w = panel(n + 6, 0)
                ends = tiles_together([bank(f) for f in range(4)], w, 512, YH, YL, 4,
                                      lambda k: pe.wait_ge(S["ret_y_split"], h * 4 + (k + 1)))
                for f, end in enumerate(ends):
                    signal(end, "ret_out_made", f == 3)
                w = panel(n + 7, 1)
                for f in range(4):
                    end = tile_of(bank(f)[:, :], w, f, 512, YH, YL, 0, 4)
                    signal(end, "ret_out_made", f == 3)
            uses.end(RET_HEADS)

            def per_layer_input(L, n):
                w = panel(n, n % 2)
                for f in range(KD):
                    end = tile_of(bank(f % 4)[:, :], w, f, 1024, PH, PL, 0, 2,
                                  wait=(lambda k: pe.wait_ge(S["ple_p_split"], 2 * L + k + 1)) if f == 0 else None)
                    signal(end, "ple_proj_made", f == KD - 1)
                    if f == 3:
                        sum_of_squares(f"post{L}")
                for j in range(4):
                    w = panel(n + 1 + j, (n + 1 + j) % 2)
                    if j == 0:
                        ends = tiles_together([bank(0), bank(1)], w, 256, HH, HL, KD,
                                              lambda k: pe.wait_ge(S["ple_h_split"], KD * L + k + 1))
                        for f, end in enumerate(ends):
                            signal(end, "ple_gate_made", f == 1)
                        continue
                    for f in range(2):
                        end = tile_of(bank((2 * j + f) % 4)[:, :], w, f, 256, HH, HL, 0, KD)
                        signal(end, "ple_gate_made", f == 1)

            per_layer_input(0, N_PLE0)

            sum_of_squares("pre1")
            for j in range(5):
                n = N_MLAIN + j
                w = panel(n, n % 2)
                if j == 0:
                    for f, end in enumerate(tiles_together([bank(0), bank(1)], w, 256, HH, HL, KD, of_h("pre1"))):
                        signal(end, "mla_in_made", f == 1)
                    continue
                for f in range(2):
                    end = tile_of(bank((2 * j + f) % 4)[:, :], w, f, 256, HH, HL, 0, KD)
                    signal(end, "mla_in_made", f == 1)
                if j == 3:
                    sum_of_squares("cq")
            sum_of_squares("ckv", TG[:, 0, :])

            with pe.Fori(0, PAIRS) as hp:
                uses.loop(hp, [5] * 4 + [4] * 4)
                n = hp * 4 + N_MLA
                s0, s1 = N_MLA % 2, (N_MLA + 1) % 2
                w = panel(n, s0)
                pe.wait_ge(S["latent_split"], KQ)
                for f in range(2):
                    tile_of(bank(f)[:, :], w, f, 256, CQH, CQL, 0, KQ).then_inc(S["mla_qk_made"], 1)
                pe.wait_ge(S["latent_split"], KQ + KC)
                for f in range(2):
                    end = tile_of(bank(2 + f)[:, :], w, f, 256, CKH, CKL, 0, KC, at=KQ * 256)
                    signal(end, "mla_qk_made", f == 1)
                w = panel(n + 1, s1)
                for f in range(2):
                    tile_of(bank(f)[:, :], w, f, 256, CQH, CQL, 0, KQ).then_inc(S["mla_qr_made"], 1)

                def latent_values(w):
                    wh, wl = w
                    for j in range(2):
                        o = bank(2 + j)
                        for t2 in range(2):
                            ts = slice(256 * j + 128 * t2, 256 * j + 128 * t2 + 128)
                            for k in range(KC):
                                c = KQ * 256 + 256 * k
                                end = mm3(o[:, 256 * t2:256 * t2 + 256], CKH[:, k, ts], CKL[:, k, ts],
                                          wh[:, c:c + 256], wl[:, c:c + 256], k == 0, k == KC - 1)
                        signal(end, "mla_v_made", j == 1)

                def scores(a):
                    rows = slice(64 * a, 64 * a + 64)
                    for qt in range(NT):
                        o, m = bank(4 + qt)[:, 0:128 * (qt + 1)], 128 * (qt + 1)
                        qs = slice(128 * qt, 128 * qt + 128)
                        mm3(o, MQH[:, a, qs], MQL[:, a, qs], MQH[:, 2 + a, 0:m], MQL[:, 2 + a, 0:m], True, False)
                        mm3(o, QRH[rows, qs], QRL[rows, qs], KRH[rows, 0:m], KRL[rows, 0:m], False, True)\
                            .then_inc(S["mla_s_made"], 1)

                def transposes(a):
                    for qt in range(NT):
                        pe.wait_ge(S["mla_p_ready"], hp * 8 + (4 * a + qt + 1))
                        o = bank(4 + qt)
                        for jt in range(qt + 1):
                            end = nc.tensor.transpose(o[:, 128 * jt:128 * jt + 128], T[:, qt, 128 * jt:128 * jt + 128], IDENT)
                        end.then_inc(S["mla_t_made"], 1)

                def weighted(a):
                    o = bank(2 + a)
                    vs = slice(128 * a, 128 * a + 128)
                    for qt in range(NT):
                        pe.wait_ge(S["mla_pt_split"], hp * 8 + (4 * a + qt + 1))
                        for jt in range(qt + 1):
                            c = 128 * (qt * (qt + 1) // 2 + jt)
                            end = mm3(o[:, 128 * qt:128 * qt + 128], MVH[:, jt, vs], MVL[:, jt, vs],
                                      PKH[:, c:c + 128], PKL[:, c:c + 128], jt == 0, jt == qt)
                    end.then_inc(S["mla_o_made"], 1)

                latent_values(w)
                pe.wait_ge(S["mla_qk_split"], hp * 4 + 4)
                pe.wait_ge(S["mla_rope_split"], hp + 2)
                scores(0)
                w = panel(n + 2, s0)
                tile_of(bank(0)[:, :], w, 0, 256, HH, HL, 0, KD).then_inc(S["mla_g_made"], 1)
                transposes(0)
                scores(1)
                pe.wait_ge(S["mla_v_split"], hp * 2 + 2)
                weighted(0)
                g1 = bank(1)
                tile_of(g1[:, :], w, 1, 256, HH, HL, 0, 4, last=False)
                transposes(1)
                tile_of(g1[:, :], w, 1, 256, HH, HL, 4, KD, first=False, at=4 * 256).then_inc(panel_used, 1)
                weighted(1)
                w = panel(n + 3, s1)
                ends = tiles_together([bank(f) for f in range(4)], w, 1024, MYH, MYL, 2,
                                      lambda k: pe.wait_ge(S["mla_y_split"], hp * 2 + (k + 1)))
                for f in range(KD):
                    end = ends[f] if f < 4 else tile_of(bank(f % 4)[:, :], w, f, 1024, MYH, MYL, 0, 2)
                    signal(end, "mla_out_made", f == KD - 1)
            uses.end(PAIRS)

            per_layer_input(1, N_PLE1)

            sum_of_squares("mix0")
            for cc in range(2):
                os_ = [bank(4 * cc + tt) for tt in range(NT)]
                for j in range(2):
                    n = N_MIX + 2 * cc + j
                    wh, wl = panel(n, n % 2)
                    for k in range(4):
                        if cc == 0:
                            of_h("mix0")(4 * j + k)
                        for tt in range(NT):
                            ts = slice(128 * tt, 128 * tt + 128)
                            end = mm3(os_[tt][:, :], HH[:, 4 * j + k, ts], HL[:, 4 * j + k, ts],
                                      wh[:, 512 * k:512 * k + 512], wl[:, 512 * k:512 * k + 512],
                                      j == 0 and k == 0, j == 1 and k == 3)
                            if k == 3 and (j == 1 or tt == NT - 1):
                                signal(end, "mix_v_made", tt == NT - 1)
            for j in range(4):
                n = N_MIX + 4 + j
                w = panel(n, n % 2)
                for f in range(2):
                    end = tile_of(bank((2 * j + f) % 4)[:, :], w, f, 256, HH, HL, 0, KD)
                    signal(end, "mix_u_made", f == 1)
            pe.wait_ge(S["wt_masked"], 1)
            for j in range(2):
                nc.tensor.matmul(bank(4 + j)[:, :], ONES[:, :], WT[:, 4 * j:4 * j + 4, :].rearrange("p g t -> p (g t)"),
                                 start=True, stop=True).then_inc(S["rowsum_made"], 1)
            pe.wait_ge(S["wt_split"], 1)
            pe.wait_ge(S["mix_split"], NT)
            for g in range(GROUPS):
                o = bank(g % 4)
                for tt in range(NT):
                    gs = slice(128 * g, 128 * g + 128)
                    end = mm3(o[:, 128 * tt:128 * tt + 128], NVH[:, tt, gs], NVL[:, tt, gs], WTH[:, g, :], WTL[:, g, :],
                              True, True)
                end.then_inc(S["mixed"], 1)
            YMH = NVH[:, :, :].rearrange("p t (g c) -> p g t c", g=GROUPS)
            YML = NVL[:, :, :].rearrange("p t (g c) -> p g t c", g=GROUPS)
            for j in range(4):
                n = N_MIX + 8 + j
                wh, wl = panel(n, n % 2)
                os_ = [bank((2 * j + f) % 4) for f in range(2)]
                for g in range(GROUPS):
                    if j == 0:
                        pe.wait_ge(S["mix_split"], NT + g + 1)
                    for f in range(2):
                        c = 256 * g + 128 * f
                        end = mm3(os_[f][:, :], wh[:, c:c + 128], wl[:, c:c + 128], YMH[:, g], YML[:, g],
                                  g == 0, g == GROUPS - 1)
                        if g == GROUPS - 1:
                            signal(end, "mix_out_made", f == 1)

            def mlp(L, n0):
                name = f"mlp{L}"
                sum_of_squares(name)
                with pe.Fori(0, CHUNKS) as c:
                    uses.loop(c, [2] * 4 + [1] * 4)
                    n = c * 4 + n0
                    for j in range(2):
                        w = panel(n + j, (n0 + j) % 2)
                        if j == 0:
                            for f, end in enumerate(tiles_together([bank(0), bank(1)], w, 256, HH, HL, KD, of_h(name))):
                                signal(end, "mlp_up_made", f == 1)
                            continue
                        for f in range(2):
                            end = tile_of(bank(2 * j + f)[:, :], w, f, 256, HH, HL, 0, KD)
                            signal(end, "mlp_up_made", f == 1)
                    for j in range(2):
                        w = panel(n + 2 + j, (n0 + j) % 2)
                        if j == 0:
                            ends = tiles_together([bank(4 + f) for f in range(4)], w, 512, HIDH, HIDL, 4,
                                                  lambda k: pe.wait_ge(S["mlp_hid_split"], c * 4 + (4 * CHUNKS * L + k + 1)))
                            for f, end in enumerate(ends):
                                signal(end, "mlp_down_made", f == 3)
                            continue
                        for f in range(4):
                            end = tile_of(bank(f)[:, :], w, f, 512, HIDH, HIDL, 0, 4)
                            signal(end, "mlp_down_made", f == 3)
                uses.end(CHUNKS)

            mlp(0, N_MLP0)

            sum_of_squares("mix1")

            def qk_tile(u, j, f):
                n = N_DIL + 3 * u + j
                end = tile_of(bank(f)[:, :], panel(n, n % 2), f, 256, HH, HL, 0, KD)
                signal(end, "dil_qk_made", f == 1)

            def values(u):
                n = N_DIL + 3 * u + 2
                wh, wl = panel(n, n % 2)
                for j in range(2):
                    o = bank(j)
                    for t2 in range(2):
                        tt = 2 * j + t2
                        if u % 3 == 0:
                            hs = [x[:, :, 128 * tt:128 * tt + 128] for x in (HH, HL)]
                        else:
                            hs = [x[:, :, :].rearrange("p k (a r) -> p k r a", r=4)[:, :, tt, :] for x in (HH, HL)]
                        for k in range(KD):
                            end = mm3(o[:, 256 * t2:256 * t2 + 256], hs[0][:, k], hs[1][:, k],
                                      wh[:, 256 * k:256 * k + 256], wl[:, 256 * k:256 * k + 256],
                                      k == 0, k == KD - 1)
                    signal(end, "dil_v_made", j == 1)

            def dil_scores(u, hh):
                pr, rows = hh // 2, slice(64 * (hh % 2), 64 * (hh % 2) + 64)
                o = bank(4 + hh % 2)
                for tt in range(NT):
                    ts = slice(128 * tt, 128 * tt + 128)
                    end = mm3(o[:, ts], DQH[rows, pr, ts], DQL[rows, pr, ts], DKH[rows, pr, ts], DKL[rows, pr, ts],
                              True, True)
                if u % 3 == 0:
                    o = bank(6 + hh % 2)
                    for tt in range(1, NT):
                        ts, ps = slice(128 * tt, 128 * tt + 128), slice(128 * tt - 128, 128 * tt)
                        end = mm3(o[:, ps], DQH[rows, pr, ts], DQL[rows, pr, ts], DKH[rows, pr, ps], DKL[rows, pr, ps],
                                  True, True)
                end.then_inc(S["dil_s_made"], 1)

            def dil_transposes(u, hh):
                t0 = 2 * (hh % 2)
                pe.wait_ge(S["dil_p_ready"], 4 * u + hh + 1)
                o = bank(4 + hh % 2)
                for tt in range(NT):
                    ts = slice(128 * tt, 128 * tt + 128)
                    end = nc.tensor.transpose(o[:, ts], T[:, t0, ts], IDENT)
                if u % 3 == 0:
                    o = bank(6 + hh % 2)
                    for tt in range(1, NT):
                        ps = slice(128 * tt - 128, 128 * tt)
                        end = nc.tensor.transpose(o[:, ps], T[:, t0 + 1, ps], IDENT)
                end.then_inc(S["dil_t_made"], 1)

            def dil_weighted(u, hh):
                pe.wait_ge(S["dil_v_split"], 2 * u + 2)
                pe.wait_ge(S["dil_pt_split"], 4 * u + hh + 1)
                o = bank(2 + hh % 2)
                vs = slice(128 * (hh // 2), 128 * (hh // 2) + 128)
                for tt in range(NT):
                    ts = slice(128 * tt, 128 * tt + 128)
                    both = u % 3 == 0 and tt > 0
                    end = mm3(o[:, ts], DVH[:, tt, vs], DVL[:, tt, vs], DPH[:, 0, ts], DPL[:, 0, ts], True, not both)
                    if both:
                        ps = slice(128 * tt - 128, 128 * tt)
                        end = mm3(o[:, ts], DVH[:, tt - 1, vs], DVL[:, tt - 1, vs], DPH[:, 1, ps], DPL[:, 1, ps],
                                  False, True)
                end.then_inc(S["dil_o_made"], 1)

            def dil_lse_rows(half):
                for pr in range(2):
                    for g in range(3):
                        o = bank(4 + g)
                        pe.wait_ge(S["dil_lse"], 6 * half + 3 * pr + g + 1)
                        for tt in range(NT):
                            ts = slice(128 * tt, 128 * tt + 128)
                            end = nc.tensor.matmul(o[:, ts], LSE_COLS[g][:, ts], IDENT, start=True, stop=True)
                        end.then_inc(S["dil_lse_made"], 1)

            w = panel(N_DIL, N_DIL % 2)
            for f, end in enumerate(tiles_together([bank(0), bank(1)], w, 256, HH, HL, KD, of_h("mix1"))):
                signal(end, "dil_qk_made", f == 1)
            for f in range(2):
                qk_tile(0, 1, f)
            for u in range(6):
                more = u < 5
                if u == 3:
                    values(u)
                    dil_lse_rows(0)
                pe.wait_ge(S["dil_qk_split"], 4 * u + 4)
                dil_scores(u, 0)
                dil_scores(u, 1)
                if u != 3:
                    values(u)
                dil_transposes(u, 0)
                dil_weighted(u, 0)
                dil_scores(u, 2)
                dil_transposes(u, 1)
                dil_weighted(u, 1)
                dil_scores(u, 3)
                if more:
                    qk_tile(u + 1, 0, 0)
                dil_transposes(u, 2)
                if more:
                    qk_tile(u + 1, 0, 1)
                dil_weighted(u, 2)
                if more:
                    qk_tile(u + 1, 1, 0)
                dil_transposes(u, 3)
                if more:
                    qk_tile(u + 1, 1, 1)
                dil_weighted(u, 3)
            dil_lse_rows(1)
            for j in range(2):
                n = N_DILOUT + j
                w = panel(n, n % 2)
                ends = tiles_together([bank(f) for f in range(4)], w, 512, DYH, DYL, 4,
                                      lambda k: pe.wait_ge(S["dil_y_split"], k + 1))
                for f, end in enumerate(ends):
                    signal(end, "dil_out_made", f == 3)

            mlp(1, N_MLP1)
            sum_of_squares("final")

        @block.scalar
        def _(act):
            def hi(dst, src):
                return nc.scalar.activation(dst, src, ACT.Copy)

            def split_panel(m, slot, half):
                act.wait_ge(raw_loaded[slot], half * 16 + 16)
                if not isinstance(m, int) or m >= 2:
                    act.wait_ge(panel_used, m - 1)
                hi(WH[:, slot, :], RAW[:, slot, :]).then_inc(hi_ready, 1)

            def split_at(m):
                split_panel(m, m % 2, m // 2)

            def split_in(i, per, m0):
                split_panel(i * per + m0, m0 % 2, i * (per // 2) + m0 // 2)

            def squares(name, n, ready):
                for k in range(n):
                    src = ready(k)
                    if k == 0:
                        nc.scalar.activation(SS[:, :], src, ACT.Square).then_inc(S["norm_sq"], 1)
                        continue
                    if k >= 3:
                        act.wait_ge(S["norm_added"], (KD - 1) * FULL.index(name) + k - 2)
                    nc.scalar.activation(SQ[:, k % 2, :], src, ACT.Square).then_inc(S["norm_sq"], 1)

            def root(name, n):
                act.wait_ge(S["norm_sum"], NORMS.index(name) + 1)
                nc.scalar.activation(R[:, :], B[4][:, :], ACT.Sqrt, bias=EPSC[:, 0:1], scale=1.0 / n)\
                    .then_inc(S["norm_root"], 1)

            def split_h(name, n, dh, before=0):
                for k in range(n):
                    act.wait_ge(S[name + "_f32"], before + k + 1)
                    hi(dh[:, k, :], T[:, k % 2, :]).then_inc(S[name + "_hi"], 1)

            def norm(name, ready, panel_behind=None):
                squares(name, KD, ready)
                root(name, D_MODEL)
                if panel_behind is not None:
                    split_at(panel_behind)
                split_h("norm", KD, HH, KD * SPLIT.index(name))

            act.dma_start(G[:, :], gains).then_inc(S["const_loaded"], 16)
            act.dma_start(CONST[:, :], consts).then_inc(S["const_loaded"], 16)
            act.dma_start(SIN1[:, :].bitcast(i32), pos).then_inc(S["pos_loaded"], 16)
            act.dma_start(X[:, :, :], xin.rearrange("k p n -> p k n")).then_inc(S["x_moved"], 16)
            act.dma_start(REL[0:32], rel).then_inc(S["rel_loaded"], 16)
            act.dma_start(ONEHOT, onehot.rearrange("b (j n) -> b j n", j=2)).then_inc(S["rel_loaded"], 16)
            split_at(0)
            act.wait_ge(S["x_moved"], 16)
            for j in range(2):
                act.wait_ge(S["bias_rows"], j + 1)
                hi(ROWS[:, j, :], B[5 + j][0:24, :]).then_inc(free[5 + j], 1)
                act.wait_ge(free[5 + j], 1)
            for kind in range(4):
                g = kind % 3
                src = ROWS8[g][:, kind // 2, 256 * (kind % 2):256 * (kind % 2) + 256]
                act.dma_start(scratch[kind], src.unsqueeze(1).to_broadcast([8, 128, 256])).then_inc(S["rows_stored"], 16)
            norm("pre0", lambda k: X[:, k, :], 1)
            for j, dst in enumerate((COS1, SIN1)):
                act.wait_ge(S["angle"], j + 1)
                nc.scalar.activation(dst[:, :], T[:, 2 + j, :], ACT.Sin).then_inc(S["sines"], 1)

            with act.Fori(0, RET_HEADS) as h:
                hs = act.snap(h * 1)
                act.dma_start(DEC[:, :], decay[bass.ds(hs, 1)].rearrange("a p n -> (a p) n")).then_inc(S["head_loaded"], 16)
                act.dma_start(GN[:, :], gn[bass.ds(hs, 1)].rearrange("a p n -> (a p) n")).then_inc(S["head_loaded"], 16)
                for j, dst in enumerate((QH, KH)):
                    for f in range(2):
                        act.wait_ge(S["ret_qk_f32"], h * 4 + (2 * j + f + 1))
                        hi(dst[:, f, :], T[:, 2 * f, :]).then_inc(S["ret_qk_hi"], 1)
                    split_in(h, 8, 2 + j)
                split_in(h, 8, 4)
                for tt in range(NT):
                    tile_done(act, "ret_v_made", tt, 4, h * 8 + 3, h * 3)
                    hi(VH[:, tt, :], B[tt][:, :]).then_inc(S["ret_v_hi"], 1)
                split_in(h, 8, 5)
                for jt in range(NT):
                    act.wait_ge(S["ret_a_f32"], h * 4 + (jt + 1))
                    m = 512 - 128 * jt
                    hi(AH[:, jt, 0:m], T[:, jt, 0:m]).then_inc(S["ret_a_hi"], 1)
                for f in range(2):
                    tile_done(act, "ret_g_made", f, 2, h * 8 + 4, h * 2)
                    nc.scalar.activation(TG[:, f, :], B[f][:, :], ACT.Tanh, scale=0.5).then_inc(S["ret_tanh"], 1)
                split_in(h, 8, 6)
                for vt in range(4):
                    act.wait_ge(S["ret_o_made"], h * 4 + (vt + 1))
                    if vt == 0:
                        dst = SS[:, :]
                    else:
                        dst = SQ[:, vt % 2, :]
                    if vt == 3:
                        act.wait_ge(S["ret_added"], h * 3 + 1)
                    nc.scalar.activation(dst, B[4 + vt][:, :], ACT.Square).then_inc(S["ret_sq"], 1)
                tile_done(act, "ret_g_made", 2, 2, h * 8 + 5, h * 2)
                act.wait_ge(S["ret_u"], h * 4 + 1)
                nc.scalar.activation(TG[:, 0, :], B[2][:, :], ACT.Tanh, scale=0.5).then_inc(S["ret_tanh"], 1)
                act.wait_ge(S["ret_sum"], h + 1)
                nc.scalar.activation(R[:, :], B[4][:, :], ACT.Sqrt, bias=EPSC[:, 1:2], scale=4.0 / RET_V)\
                    .then_inc(S["ret_root"], 1)
                tile_done(act, "ret_g_made", 3, 2, h * 8 + 5, h * 2)
                act.wait_ge(S["ret_u"], h * 4 + 2)
                nc.scalar.activation(TG[:, 1, :], B[3][:, :], ACT.Tanh, scale=0.5).then_inc(S["ret_tanh"], 1)
                split_in(h, 8, 7)
                for vt in range(4):
                    act.wait_ge(S["ret_y_f32"], h * 4 + (vt + 1))
                    hi(YH[:, vt, :], O[:, vt, :]).then_inc(S["ret_y_hi"], 1)
                split_in(h, 8, 8)
                split_in(h, 8, 9)

            def per_layer_input(L, n):
                act.wait_ge(S["ple_begin"], L + 1)
                act.dma_start(PF[:, :, :], pin[L].rearrange("k p n -> p k n")).then_inc(S["p_loaded"], 16)
                act.wait_ge(S["p_loaded"], 16 * L + 16)
                for k in range(2):
                    hi(PH[:, k, :], PF[:, k, :]).then_inc(S["ple_p_hi"], 1)
                if L == 1:
                    split_at(n + 1)
                squares(f"post{L}", KD, lambda k: ACC[:, k, :])
                for f in range(KD):
                    tile_done(act, "ple_proj_made", f, KD, n, base=7 * L)
                    hi(PJ[:, f, :], B[f % 4][:, :]).then_inc(free[f % 4], 1)
                    if f == 3:
                        root(f"post{L}", D_MODEL)
                for k in range(KD):
                    act.wait_ge(S["ple_x_new"], KD * L + k + 1)
                    hi(HH[:, k, :], X[:, k, :]).then_inc(S["ple_hi"], 1)
                for f in range(KD):
                    if f % 2 == 0:
                        split_at(n + 2 + f // 2)
                    tile_done(act, "ple_gate_made", f, 2, n + 1 + f // 2, base=4 * L)
                    if f >= 2:
                        act.wait_ge(S["ple_mixed"], KD * L + f - 1)
                    nc.scalar.activation(TG[:, f % 2, :], B[f % 4][:, :], ACT.Tanh, scale=0.5).then_inc(S["ple_tanh"], 1)

            def updated(sig, before=0):
                def ready(k):
                    act.wait_ge(S[sig], before + k + 1)
                    return X[:, k, :]
                return ready

            per_layer_input(0, N_PLE0)
            norm("pre1", updated("ple_done"), N_MLAIN + 1)
            act.dma_start(xsave.rearrange("k p n -> p k n"), X[:, :, :]).then_inc(S["x_moved"], 16)
            act.wait_ge(S["x_moved"], 32)
            act.dma_start(SIN2[:, :].bitcast(i32), pos).then_inc(S["pos_loaded"], 16)
            for f in range(KQ + KC):
                tile_done(act, "mla_in_made", f, 2, N_MLAIN + f // 2)
                hi(ACC[:, f, :], B[f % 4][:, :])
                if f >= KQ:
                    dst = TG[:, f - KQ, :]
                elif f == 0:
                    dst = SS[:, :]
                else:
                    dst = SQ[:, f % 2, :]
                    if f >= 3:
                        act.wait_ge(S["cq_added"], f - 2)
                nc.scalar.activation(dst, B[f % 4][:, :], ACT.Square).then_inc(S["mla_sq"], 1)
                act.drain().then_inc(free[f % 4], 1)
                if f % 2 == 1:
                    split_at(N_MLAIN + 2 + f // 2)
            for j, dst in enumerate((COS2, SIN2)):
                act.wait_ge(S["angle"], j + 3)
                nc.scalar.activation(dst[:, :], T[:, 2 + j, :], ACT.Sin).then_inc(S["sines"], 1)
            root("cq", Q_LORA)
            split_h("latent", KQ, CQH)
            act.wait_ge(S["mla_rope_f32"], 1)
            hi(KRH[:, :], T[:, 2, :]).then_inc(S["mla_rope_hi"], 1)
            root("ckv", KV_LORA)
            split_h("latent", KC, CKH, KQ)

            with act.Fori(0, PAIRS) as hp:
                split_in(hp, 4, N_MLA + 1)
                for f in range(4):
                    tile_done(act, "mla_qk_made", f, 4, hp * 4 + N_MLA, hp * 3)
                    hi(MQH[:, f, :], B[f][:, :]).then_inc(S["mla_qk_hi"], 1)
                split_in(hp, 4, N_MLA + 2)
                act.wait_ge(S["mla_rope_f32"], hp + 2)
                hi(QRH[:, :], T[:, 0, :]).then_inc(S["mla_rope_hi"], 1)

                def high_values():
                    for j in range(2):
                        tile_done(act, "mla_v_made", j, 2, hp * 4 + (N_MLA + 1), hp * 1)
                        hi(MVH[:, 2 * j:2 * j + 2, :].rearrange("p t n -> p (t n)"), B[2 + j][:, :])\
                            .then_inc(S["mla_v_hi"], 1)
                    split_in(hp, 4, N_MLA + 3)

                def exponentials(a):
                    for qt in range(NT):
                        m = 128 * (qt + 1)
                        act.wait_ge(S["mla_max"], hp * 8 + (4 * a + qt + 1))
                        if a == 1:
                            act.wait_ge(S["mla_t_made"], hp * 8 + (qt + 1))
                        nc.scalar.activation(T[:, qt, 0:m], B[4 + qt][:, 0:m], ACT.Exp, bias=ST[:, 1, qt:qt + 1],
                                             scale=MLA_SCALE, accum_out=ST[:, 2, qt:qt + 1]).then_inc(S["mla_exp"], 1)

                def high_probabilities(a):
                    for qt in range(NT):
                        act.wait_ge(S["mla_t_made"], hp * 8 + (4 * a + qt + 1))
                        c, m = 128 * (qt * (qt + 1) // 2), 128 * (qt + 1)
                        hi(PKH[:, c:c + m], B[4 + qt][:, 0:m]).then_inc(S["mla_pt_hi"], 1)

                def tanh_gate(a):
                    tile_done(act, "mla_g_made", a, 2, hp * 4 + (N_MLA + 2), hp * 1)
                    nc.scalar.activation(TG[:, a, :], B[a][:, :], ACT.Tanh, scale=0.5).then_inc(S["mla_tanh"], 1)

                def high_y(a):
                    act.wait_ge(S["mla_y_f32"], hp * 2 + (a + 1))
                    hi(MYH[:, a, :], SQ[:, a, :]).then_inc(S["mla_y_hi"], 1)

                high_values()
                exponentials(0)
                high_probabilities(0)
                exponentials(1)
                tanh_gate(0)
                high_y(0)
                high_probabilities(1)
                tanh_gate(1)
                high_y(1)
                split_in(hp, 4, N_MLA + 4)

            act.wait_ge(S["ple_begin"], 2)
            act.dma_start(X[:, :, :], xsave.rearrange("k p n -> p k n")).then_inc(S["x_moved"], 16)
            per_layer_input(1, N_PLE1)
            norm("mix0", updated("ple_done", KD), N_MIX + 1)

            act.dma_start(WT[:, :, :], wsT).then_inc(S["ws_loaded"], 16)
            act.dma_start(BS[:, :, :], bs).then_inc(S["ws_loaded"], 16)
            for cc in range(2):
                split_at(N_MIX + 2 + 2 * cc)
                for tt in range(NT):
                    tile_done(act, "mix_v_made", 4 * cc + tt, 4, N_MIX + 2 * cc + 1)
                    nc.scalar.activation(NV[:, tt, 512 * cc:512 * cc + 512], B[4 * cc + tt][:, :], ACT.Gelu,
                                         accum_out=ST[:, cc, tt:tt + 1]).then_inc(free[4 * cc + tt], 1)
                    act.drain().then_inc(S["mix_gelu"], 1)
                split_at(N_MIX + 3 + 2 * cc)
            for tt in range(NT):
                act.drain()
                act.wait_ge(S["nv_centred"], tt + 1)
                nc.scalar.activation(SQ[:, :, :].rearrange("p a n -> p (a n)"), NV[:, tt, :], ACT.Square,
                                     accum_out=ST[:, 4, tt:tt + 1]).then_inc(S["nv_var"], 1)
            act.wait_ge(S["nv_var"], NT)
            nc.scalar.activation(ST[:, 5, :], ST[:, 4, :], ACT.Sqrt, bias=EPSC[:, 0:1], scale=1.0 / 1024)\
                .then_inc(S["nv_root"], 1)
            for tt in range(NT):
                act.wait_ge(S["mix_f32"], tt + 1)
                hi(NVH[:, tt, :], NV[:, tt, :]).then_inc(S["mix_hi"], 1)
            act.wait_ge(S["wt_masked"], 1)
            hi(WTH[:, :, :], WT[:, :, :]).then_inc(S["wt_hi"], 1)
            for f in range(8):
                tile_done(act, "mix_u_made", f, 2, N_MIX + 4 + f // 2)
                nc.scalar.activation(GU[:, f, :], B[f % 4][:, :], ACT.Gelu).then_inc(free[f % 4], 1)
                if f % 2 == 1 and f < 7:
                    split_at(N_MIX + 6 + f // 2)
            act.drain().then_inc(S["mix_u"], 1)
            split_at(N_MIX + 9)
            for g in range(GROUPS):
                act.wait_ge(S["mix_f32"], NT + g + 1)
                hi(NVH[:, :, 128 * g:128 * g + 128], T[:, g % 2, :].rearrange("p (t n) -> p t n", t=NT))\
                    .then_inc(S["mix_hi"], 1)
            for j in range(3):
                split_at(N_MIX + 10 + j)

            def mlp(L, n0):
                at = 4 * CHUNKS * L

                def chunk(c, next_panel=True):
                    split_in(c, 4, n0 + 1)
                    for j in range(2):
                        for f in range(2 * j, 2 * j + 2):
                            tile_done(act, "mlp_up_made", f, 2, c * 4 + (n0 + f // 2), c * 2, 2 * CHUNKS * L)
                            if f >= 2:
                                act.wait_ge(S["mlp_hid_f32"], c * 4 + (at + f - 1))
                            nc.scalar.activation(TG[:, f % 2, :], B[f][:, :], ACT.Relu).then_inc(S["mlp_relu"], 1)
                            act.drain().then_inc(free[f], 1)
                        for f in range(2 * j, 2 * j + 2):
                            act.wait_ge(S["mlp_hid_f32"], c * 4 + (at + f + 1))
                            hi(HIDH[:, f, :], T[:, f, :]).then_inc(S["mlp_hid_hi"], 1)
                        split_in(c, 4, n0 + 2 + j)
                    if next_panel:
                        split_in(c, 4, n0 + 4)

                if L == 0:
                    with act.Fori(0, CHUNKS) as c:
                        chunk(c)
                else:
                    with act.Fori(0, CHUNKS - 1) as c:
                        chunk(c)
                    chunk(CHUNKS - 1, next_panel=False)

            norm("mlp0", updated("mix_done"))
            mlp(0, N_MLP0)

            norm("mix1", updated("mlp_done"), N_DIL + 1)
            act.wait_ge(S["rows_stored"], 64)
            for kind in range(4):
                rows = scratch[kind].rearrange("h q y -> h (q y)")[:, 127:127 + 128 * 255]
                tile = rows.rearrange("h (q y) -> q h y", y=255)[:, :, 0:128]
                act.dma_start(TAB[:, kind], tile).then_inc(S["tab_loaded"], 16)

            def high_qk(u, f):
                tile_done(act, "dil_qk_made", f, 2, N_DIL + 3 * u + f // 2, 2 * u)
                dst = (DQH if f < 2 else DKH)[:, f % 2, :]
                hi(in_order(dst, u % 3), natural(B[f % 2], u % 3)).then_inc(S["dil_qk_hi"], 1)

            def high_values(u):
                for j in range(2):
                    tile_done(act, "dil_v_made", j, 2, N_DIL + 3 * u + 2, u)
                    hi(DVH[:, 2 * j:2 * j + 2, :].rearrange("p t n -> p (t n)"), B[j][:, :]).then_inc(S["dil_v_hi"], 1)
                split_at(N_DIL + 3 * u + 4)

            def exponentials(u, hh):
                t0 = 2 * (hh % 2)
                act.wait_ge(S["dil_centred"], 4 * u + hh + 1)
                nc.scalar.activation(T[:, t0, :], T[:, t0, :], ACT.Exp)
                if u % 3 == 0:
                    nc.scalar.activation(T[:, t0 + 1, 0:384], T[:, t0 + 1, 0:384], ACT.Exp)
                act.drain().then_inc(S["dil_exp"], 1)

            def high_probabilities(u, hh):
                act.wait_ge(S["dil_t_made"], 4 * u + hh + 1)
                hi(DPH[:, 0, :], B[4 + hh % 2][:, :])
                if u % 3 == 0:
                    hi(DPH[:, 1, 0:384], B[6 + hh % 2][:, 0:384])
                act.drain().then_inc(S["dil_pt_hi"], 1)

            def head_result(u, hh):
                g = u % 3
                act.wait_ge(S["dil_o_made"], 4 * u + hh + 1)
                rows = slice(64 * (hh % 2), 64 * (hh % 2) + 64)
                hi(natural(OG[hh // 2][rows, g, :], g), in_order(B[2 + hh % 2][rows, :], g)).then_inc(free[2 + hh % 2], 1)

            def combine(half, between):
                act.wait_ge(S["dil_sums"], half + 1)
                nc.scalar.activation(SUMS[:, :, :, :].rearrange("p a b c -> p (a b c)"),
                                     SUMS[:, :, :, :].rearrange("p a b c -> p (a b c)"), ACT.Ln).then_inc(S["dil_ln"], 1)
                if between is not None:
                    high_values(between)
                for pr in range(2):
                    v = 2 * half + pr
                    for g in range(3):
                        act.wait_ge(S["dil_lse_made"], 3 * v + g + 1)
                        hi(natural(LSE[:, g, :], g), in_order(B[4 + g][:, :], g)).then_inc(free[4 + g], 1)
                    act.drain().then_inc(S["dil_lse_copied"], 1)
                    act.wait_ge(S["dil_lse_centred"], v + 1)
                    nc.scalar.activation(LSE, LSE, ACT.Exp).then_inc(S["dil_weights"], 1)
                    act.wait_ge(S["dil_y_f32"], v + 1)
                    hi(DYH[:, v, :], DY).then_inc(S["dil_y_hi"], 1)

            for f in range(4):
                high_qk(0, f)
                if f % 2 == 1:
                    split_at(N_DIL + 2 + f // 2)
            for u in range(6):
                more = u < 5
                if u == 3:
                    combine(0, u)
                exponentials(u, 0)
                exponentials(u, 1)
                if u != 3:
                    high_values(u)
                high_probabilities(u, 0)
                head_result(u, 0)
                high_probabilities(u, 1)
                head_result(u, 1)
                exponentials(u, 2)
                if more:
                    high_qk(u + 1, 0)
                exponentials(u, 3)
                high_probabilities(u, 2)
                if more:
                    high_qk(u + 1, 1)
                    split_at(N_DIL + 3 * u + 5)
                head_result(u, 2)
                if more:
                    high_qk(u + 1, 2)
                high_probabilities(u, 3)
                if more:
                    high_qk(u + 1, 3)
                    split_at(N_DIL + 3 * u + 6)
                head_result(u, 3)
            combine(1, None)
            split_at(N_DILOUT + 2)
            norm("mlp1", updated("dil_done"))
            mlp(1, N_MLP1)
            squares("final", KD, updated("mlp_done", KD))
            root("final", D_MODEL)

        @block.vector
        def _(ve):
            v = nc.vector

            def lo(dst, src, high):
                return v.tensor_tensor(dst, src, high.bitcast(f32), ALU.subtract)

            def gain(name, k):
                c = GAIN_AT[name] + k
                return G[:, c:c + 1]

            def add_squares(name, n):
                for k in range(1, n):
                    ve.wait_ge(S["norm_sq"], n * FULL.index(name) + k + 1)
                    if k > 1:
                        ve.drain()
                    v.tensor_tensor(SS[:, :], SS[:, :], SQ[:, k % 2, :], ALU.add).then_inc(S["norm_added"], 1)
                ve.drain().then_inc(S["norm_squares"], 1)

            def inverse_root(name):
                ve.wait_ge(S["norm_root"], NORMS.index(name) + 1)
                v.reciprocal(R[:, :], R[:, :]).then_inc(free[4], 1)
                ve.drain()

            def scaled(name, n, src, gains_of, dh, dl, sig, before=0):
                for k in range(n + 1):
                    if k < n:
                        ve.drain()
                        v.scalar_tensor_tensor(T[:, k % 2, :], src[:, k, :], gain(gains_of[0], gains_of[1] + k), R[:, :],
                                               ALU.mult, ALU.mult).then_inc(S[name + "_f32"], 1)
                    if k > 0:
                        ve.wait_ge(S[name + "_hi"], before + k)
                        lo(dl[:, k - 1, :], T[:, (k - 1) % 2, :], dh[:, k - 1, :]).then_inc(S[sig], 1)

            def norm(name):
                add_squares(name, KD)
                inverse_root(name)
                scaled("norm", KD, X, (name, 0), HH, HL, "norm_h_split", KD * SPLIT.index(name))

            def angles(use, positions, freq, between=lambda step: None):
                t = [T[:, j, :] for j in range(4)]
                MAGIC = 1.5 * 2.0 ** 23
                ve.drain()
                ve.wait_ge(S["pos_loaded"], 16 * use)
                v.tensor_scalar(t[0], positions, freq, None, ALU.mult)

                def less(dst, src, per_turn, shift, parts):
                    ve.drain()
                    v.tensor_scalar(t[1], src, per_turn, shift, ALU.mult, ALU.add)
                    ve.drain()
                    v.tensor_scalar(t[1], t[1], MAGIC, MAGIC, ALU.add, ALU.subtract)
                    for part in parts:
                        ve.drain()
                        v.scalar_tensor_tensor(dst, t[1], -part, src, ALU.mult, ALU.add)
                        src = dst
                    ve.drain()

                turns = TWO_PI * COARSE
                less(t[0], t[0], 1.0 / turns, 0.0, _parts(turns, 7, 6))
                for step, (dst, quarter) in enumerate(((t[2], 0.25), (t[3], 0.0))):
                    between(step)
                    less(dst, t[0], 1.0 / TWO_PI, quarter, _parts(TWO_PI, 8, 5))
                    v.tensor_scalar(dst, dst, quarter * TWO_PI, 3.1415925, ALU.add, ALU.min)
                    ve.drain()
                    v.tensor_scalar(dst, dst, -3.1415925, None, ALU.max).then_inc(S["angle"], 1)

            for b in BankUses.GIVEN:
                ve.drain().then_inc(free[b], 1)
            v.memset(ONES[:, :], 1.0)
            v.memset(EPSC[:, 0:1], EPS)
            v.memset(EPSC[:, 1:2], 4 * EPS)
            v.memset(REL[32:33, :], NEG)
            ve.drain().then_inc(S["rel_neg"], 1)
            ve.wait_ge(S["const_loaded"], 32)
            angles(1, SIN1[:, :].bitcast(i32), FREQ1)
            norm("pre0")
            ve.wait_ge(S["rows_stored"], 64)
            v.memset(ACC[:, :, :], 0.0)
            ve.wait_ge(S["sines"], 2)

            with ve.Fori(0, RET_HEADS) as h:
                for b, dh, dl in ((0, QH, QL), (2, KH, KL)):
                    ve.drain()
                    ve.wait_ge(panel_used, h * 8 + (1 + b // 2))
                    v.tensor_tensor(T[:, 0, :], B[b][:, :], COS1[:, :], ALU.mult)
                    v.tensor_tensor(T[:, 1, :], B[b + 1][:, :], SIN1[:, :], ALU.mult)
                    v.tensor_tensor(T[:, 2, :], B[b + 1][:, :], COS1[:, :], ALU.mult).then_inc(free[b + 1], 1)
                    v.tensor_tensor(T[:, 3, :], B[b][:, :], SIN1[:, :], ALU.mult).then_inc(free[b], 1)
                    ve.drain()
                    v.tensor_tensor(T[:, 0, :], T[:, 0, :], T[:, 1, :], ALU.subtract).then_inc(S["ret_qk_f32"], 1)
                    v.tensor_tensor(T[:, 2, :], T[:, 2, :], T[:, 3, :], ALU.add).then_inc(S["ret_qk_f32"], 1)
                    for f in range(2):
                        ve.wait_ge(S["ret_qk_hi"], h * 4 + (b + f + 1))
                        lo(dl[:, f, :], T[:, 2 * f, :], dh[:, f, :]).then_inc(S["ret_qk_split"], 1)
                for tt in range(NT):
                    ve.wait_ge(S["ret_v_hi"], h * 4 + (tt + 1))
                    lo(VL[:, tt, :], B[tt][:, :], VH[:, tt, :]).then_inc(S["ret_v_split"], 1)
                    ve.drain().then_inc(free[tt], 1)
                ve.drain()
                ve.wait_ge(S["head_loaded"], h * 32 + 32)
                for jt in range(NT):
                    m = 512 - 128 * jt
                    ve.wait_ge(S["ret_a_made"], h * 4 + (jt + 1))
                    v.tensor_tensor(T[:, jt, 0:m], B[4 + jt][:, 0:m], DEC[:, 0:m], ALU.mult).then_inc(S["ret_a_f32"], 1)
                    ve.drain().then_inc(free[4 + jt], 1)
                for jt in range(NT):
                    m = 512 - 128 * jt
                    ve.wait_ge(S["ret_a_hi"], h * 4 + (jt + 1))
                    lo(AL[:, jt, 0:m], T[:, jt, 0:m], AH[:, jt, 0:m]).then_inc(S["ret_a_split"], 1)

                def twice_silu(f):
                    ve.wait_ge(S["ret_tanh"], h * 4 + (f + 1))
                    v.scalar_tensor_tensor(U[:, f, :], TG[:, f % 2, :], 1.0, B[f][:, :], ALU.add, ALU.mult)\
                        .then_inc(S["ret_u"], 1)
                    ve.drain().then_inc(free[f], 1)

                twice_silu(0)
                twice_silu(1)
                for vt in range(4):
                    ve.wait_ge(S["ret_sq"], h * 4 + (vt + 1))
                    v.tensor_scalar(O[:, vt, :], B[4 + vt][:, :], GN[:, vt:vt + 1], None, ALU.mult).then_inc(free[4 + vt], 1)
                    if vt > 0:
                        v.tensor_tensor(SS[:, :], SS[:, :], SQ[:, vt % 2, :], ALU.add).then_inc(S["ret_added"], 1)
                        ve.drain()
                ve.drain().then_inc(S["ret_squares"], 1)
                for vt in range(2):
                    v.tensor_tensor(O[:, vt, :], O[:, vt, :], U[:, vt, :], ALU.mult)
                ve.drain()
                twice_silu(2)
                ve.wait_ge(S["ret_root"], h + 1)
                v.reciprocal(R[:, :], R[:, :]).then_inc(free[4], 1)
                ve.drain()
                for vt in range(2):
                    v.tensor_tensor(O[:, vt, :], O[:, vt, :], R[:, :], ALU.mult).then_inc(S["ret_y_f32"], 1)
                v.tensor_tensor(O[:, 2, :], O[:, 2, :], R[:, :], ALU.mult)
                v.tensor_tensor(O[:, 3, :], O[:, 3, :], R[:, :], ALU.mult)
                ve.drain()
                v.tensor_tensor(O[:, 2, :], O[:, 2, :], U[:, 2, :], ALU.mult).then_inc(S["ret_y_f32"], 1)
                twice_silu(3)
                v.tensor_tensor(O[:, 3, :], O[:, 3, :], U[:, 3, :], ALU.mult).then_inc(S["ret_y_f32"], 1)
                for vt in range(4):
                    ve.wait_ge(S["ret_y_hi"], h * 4 + (vt + 1))
                    lo(YL[:, vt, :], O[:, vt, :], YH[:, vt, :]).then_inc(S["ret_y_split"], 1)
                for f in range(KD):
                    tile_done(ve, "ret_out_made", f, 4, h * 8 + (6 + f // 4), h * 6)
                    v.tensor_tensor(ACC[:, f, :], ACC[:, f, :], B[f % 4][:, :], ALU.add).then_inc(free[f % 4], 1)

            def per_layer_input(L):
                post = f"post{L}"
                ve.drain().then_inc(S["ple_begin"], 1)
                for k in range(2):
                    ve.wait_ge(S["ple_p_hi"], 2 * L + k + 1)
                    lo(PL[:, k, :], PF[:, k, :], PH[:, k, :]).then_inc(S["ple_p_split"], 1)
                add_squares(post, KD)
                if L == 1:
                    ve.wait_ge(S["x_moved"], 48)
                inverse_root(post)
                for k in range(KD + 2):
                    if k < KD:
                        ve.drain()
                        v.scalar_tensor_tensor(T[:, k % 2, :], ACC[:, k, :], gain(post, k), R[:, :], ALU.mult, ALU.mult)
                        ve.drain()
                        v.tensor_tensor(X[:, k, :], X[:, k, :], T[:, k % 2, :], ALU.add).then_inc(S["ple_x_new"], 1)
                    if 0 < k <= KD:
                        ve.wait_ge(S["ple_hi"], KD * L + k)
                        lo(HL[:, k - 1, :], X[:, k - 1, :], HH[:, k - 1, :]).then_inc(S["ple_h_split"], 1)
                for f in range(KD):
                    ve.wait_ge(S["ple_tanh"], KD * L + f + 1)
                    ve.drain()
                    v.scalar_tensor_tensor(T[:, f % 2, :], TG[:, f % 2, :], 1.0, PJ[:, f, :], ALU.add, ALU.mult)\
                        .then_inc(S["ple_mixed"], 1)
                    ve.drain().then_inc(free[f % 4], 1)
                    v.scalar_tensor_tensor(X[:, f, :], T[:, f % 2, :], 0.5, X[:, f, :], ALU.mult, ALU.add)\
                        .then_inc(S["ple_done"], 1)

            per_layer_input(0)
            norm("pre1")

            def add_query_squares(step):
                for f in ((1,), (2,), (3, 4, 5))[step]:
                    ve.drain()
                    ve.wait_ge(S["mla_sq"], f + 1)
                    v.tensor_tensor(SS[:, :], SS[:, :], SQ[:, f % 2, :], ALU.add).then_inc(S["cq_added"], 1)

            angles(2, SIN2[:, :].bitcast(i32), FREQ2, add_query_squares)
            add_query_squares(2)
            ve.drain().then_inc(S["norm_squares"], 1)
            ve.wait_ge(S["mla_sq"], KQ + KC)
            v.tensor_tensor(TG[:, 0, :], TG[:, 0, :], TG[:, 1, :], ALU.add).then_inc(S["norm_squares"], 1)
            ve.wait_ge(S["sines"], 4)
            v.tensor_scalar(SIN2[:, :], SIN2[:, :], SIGN, None, ALU.mult)
            inverse_root("cq")
            scaled("latent", KQ, ACC, ("qn", 0), CQH, CQL, "latent_split")
            ve.wait_ge(panel_used, N_MLAIN + 5)
            v.tensor_tensor(T[:, 2, :], B[0][:, :], COS2[:, :], ALU.mult).then_inc(free[0], 1)
            v.tensor_tensor(T[:, 3, :], B[1][:, :], SIN2[:, :], ALU.mult).then_inc(free[1], 1)
            ve.drain()
            v.tensor_tensor(T[:, 2, :], T[:, 2, :], T[:, 3, :], ALU.add).then_inc(S["mla_rope_f32"], 1)
            ve.wait_ge(S["mla_rope_hi"], 1)
            lo(KRL[:, :], T[:, 2, :], KRH[:, :]).then_inc(S["mla_rope_split"], 1)
            inverse_root("ckv")
            scaled("latent", KC, ACC[:, KQ:KQ + KC, :], ("kvn", 0), CKH, CKL, "latent_split", KQ)
            v.memset(ACC[:, :, :], 0.0)
            ve.drain()

            with ve.Fori(0, PAIRS) as hp:
                for f in range(4):
                    ve.wait_ge(S["mla_qk_hi"], hp * 4 + (f + 1))
                    lo(MQL[:, f, :], B[f][:, :], MQH[:, f, :]).then_inc(S["mla_qk_split"], 1)
                    ve.drain().then_inc(free[f], 1)
                ve.drain()
                ve.wait_ge(S["mla_qr_made"], hp * 2 + 2)
                v.tensor_tensor(T[:, 0, :], B[0][:, :], COS2[:, :], ALU.mult).then_inc(free[0], 1)
                v.tensor_tensor(T[:, 1, :], B[1][:, :], SIN2[:, :], ALU.mult).then_inc(free[1], 1)
                ve.drain()
                v.tensor_tensor(T[:, 0, :], T[:, 0, :], T[:, 1, :], ALU.add).then_inc(S["mla_rope_f32"], 1)
                ve.wait_ge(S["mla_rope_hi"], hp + 2)
                lo(QRL[:, :], T[:, 0, :], QRH[:, :]).then_inc(S["mla_rope_split"], 1)

                def low_values():
                    for j in range(2):
                        ve.wait_ge(S["mla_v_hi"], hp * 2 + (j + 1))
                        vj = slice(2 * j, 2 * j + 2)
                        lo(MVL[:, vj, :].rearrange("p t n -> p (t n)"), B[2 + j][:, :],
                           MVH[:, vj, :].rearrange("p t n -> p (t n)")).then_inc(S["mla_v_split"], 1)
                        ve.drain().then_inc(free[2 + j], 1)

                def maxima(a):
                    for qt in range(NT):
                        ve.wait_ge(S["mla_s_made"], hp * 8 + (4 * a + qt + 1))
                        d = B[4 + qt][:, 128 * qt:128 * qt + 128]
                        v.tensor_tensor(d, d, CAUSAL, ALU.add)
                        ve.drain()
                        v.reduce_max(ST[:, 0, qt:qt + 1], B[4 + qt][:, 0:128 * (qt + 1)], AX.X)
                        ve.drain()
                        v.tensor_scalar(ST[:, 1, qt:qt + 1], ST[:, 0, qt:qt + 1], -MLA_SCALE, None, ALU.mult)\
                            .then_inc(S["mla_max"], 1)

                def probabilities(a):
                    for qt in range(NT):
                        m = 128 * (qt + 1)
                        ve.wait_ge(S["mla_exp"], hp * 8 + (4 * a + qt + 1))
                        v.reciprocal(ST[:, 3, qt:qt + 1], ST[:, 2, qt:qt + 1])
                        ve.drain()
                        v.tensor_scalar(T[:, qt, 0:m], T[:, qt, 0:m], ST[:, 3, qt:qt + 1], None, ALU.mult)\
                            .then_inc(S["mla_p_ready"], 1)
                        ve.drain().then_inc(free[4 + qt], 1)

                def low_probabilities(a):
                    for qt in range(NT):
                        ve.wait_ge(S["mla_pt_hi"], hp * 8 + (4 * a + qt + 1))
                        c, m = 128 * (qt * (qt + 1) // 2), 128 * (qt + 1)
                        lo(PKL[:, c:c + m], B[4 + qt][:, 0:m], PKH[:, c:c + m]).then_inc(S["mla_pt_split"], 1)
                        ve.drain().then_inc(free[4 + qt], 1)

                def twice_silu(a):
                    ve.wait_ge(S["mla_tanh"], hp * 2 + (a + 1))
                    v.scalar_tensor_tensor(MU[:, a, :], TG[:, a, :], 1.0, B[a][:, :], ALU.add, ALU.mult).then_inc(free[a], 1)
                    ve.drain()

                def gated(a):
                    ve.wait_ge(S["mla_o_made"], hp * 2 + (a + 1))
                    v.scalar_tensor_tensor(SQ[:, a, :], B[2 + a][:, :], 0.5, MU[:, a, :], ALU.mult, ALU.mult)\
                        .then_inc(S["mla_y_f32"], 1)
                    ve.drain().then_inc(free[2 + a], 1)

                def low_y(a):
                    ve.wait_ge(S["mla_y_hi"], hp * 2 + (a + 1))
                    lo(MYL[:, a, :], SQ[:, a, :], MYH[:, a, :]).then_inc(S["mla_y_split"], 1)

                low_values()
                maxima(0)
                probabilities(0)
                low_probabilities(0)
                maxima(1)
                probabilities(1)
                twice_silu(0)
                gated(0)
                low_y(0)
                low_probabilities(1)
                twice_silu(1)
                gated(1)
                low_y(1)
                for f in range(KD):
                    tile_done(ve, "mla_out_made", f, KD, hp * 4 + (N_MLA + 3), hp * 7)
                    v.tensor_tensor(ACC[:, f, :], ACC[:, f, :], B[f % 4][:, :], ALU.add).then_inc(free[f % 4], 1)

            per_layer_input(1)
            norm("mix0")

            mean, root, inv = ST[:, 2, :], ST[:, 5, :], ST[:, 3, :]
            ve.wait_ge(S["ws_loaded"], 32)
            v.tensor_tensor(WT[:, :, :], WT[:, :, :], UPPER.unsqueeze(1).to_broadcast([128, GROUPS, 128]), ALU.mult)\
                .then_inc(S["wt_masked"], 1)
            ve.wait_ge(S["mix_gelu"], 8)
            v.tensor_tensor(mean, ST[:, 0, :], ST[:, 1, :], ALU.add)
            ve.drain()
            v.tensor_scalar(mean, mean, 1.0 / 1024, None, ALU.mult)
            ve.drain()
            for tt in range(NT):
                v.tensor_scalar(NV[:, tt, :], NV[:, tt, :], mean[:, tt:tt + 1], None, ALU.subtract)\
                    .then_inc(S["nv_centred"], 1)
            ve.wait_ge(S["nv_root"], 1)
            v.reciprocal(inv, root)
            ve.drain()
            for tt in range(NT):
                v.tensor_scalar(NV[:, tt, :], NV[:, tt, :], inv[:, tt:tt + 1], None, ALU.mult).then_inc(S["mix_f32"], 1)
            for tt in range(NT):
                ve.wait_ge(S["mix_hi"], tt + 1)
                lo(NVL[:, tt, :], NV[:, tt, :], NVH[:, tt, :]).then_inc(S["mix_split"], 1)
            ve.wait_ge(S["wt_hi"], 1)
            lo(WTL[:, :, :], WT[:, :, :], WTH[:, :, :]).then_inc(S["wt_split"], 1)
            for j in range(2):
                ve.wait_ge(S["rowsum_made"], j + 1)
                for g in range(4 * j, 4 * j + 4):
                    end = v.scalar_tensor_tensor(BT[:, g, :], B[4 + j][:, 128 * (g % 4):128 * (g % 4) + 128], gain("lnb", g),
                                                 BS[:, g, :], ALU.mult, ALU.add)
                end.then_inc(free[4 + j], 1)
            ve.wait_ge(S["mix_u"], 1)

            def tokens(t):
                return t.rearrange("p (t n) -> p t n", t=NT)

            for g in range(GROUPS + 1):
                if g < GROUPS:
                    ve.drain()
                    ve.wait_ge(S["mixed"], g + 1)
                    v.scalar_tensor_tensor(tokens(T[:, g % 2, :]), tokens(B[g % 4][:, :]), gain("lng", g),
                                           BT[:, g, :].unsqueeze(1).to_broadcast([128, NT, 128]), ALU.mult, ALU.add)\
                        .then_inc(free[g % 4], 1)
                    ve.drain()
                    v.tensor_tensor(T[:, g % 2, :], T[:, g % 2, :], GU[:, g, :], ALU.mult).then_inc(S["mix_f32"], 1)
                if g > 0:
                    ve.wait_ge(S["mix_hi"], NT + g)
                    gs = slice(128 * (g - 1), 128 * g)
                    lo(NVL[:, :, gs], tokens(T[:, (g - 1) % 2, :]), NVH[:, :, gs]).then_inc(S["mix_split"], 1)
            for f in range(KD):
                tile_done(ve, "mix_out_made", f, 2, N_MIX + 8 + f // 2)
                v.tensor_tensor(X[:, f, :], X[:, f, :], B[f % 4][:, :], ALU.add).then_inc(S["mix_done"], 1)
                ve.drain().then_inc(free[f % 4], 1)

            def mlp(L, n0):
                at = 4 * CHUNKS * L

                def chunk(c, last):
                    for j in range(2):
                        for f in range(2 * j, 2 * j + 2):
                            ve.drain()
                            ve.wait_ge(S["mlp_relu"], c * 4 + (at + f + 1))
                            v.tensor_tensor(T[:, f, :], TG[:, f % 2, :], TG[:, f % 2, :], ALU.mult)\
                                .then_inc(S["mlp_hid_f32"], 1)
                        for f in range(2 * j, 2 * j + 2):
                            ve.wait_ge(S["mlp_hid_hi"], c * 4 + (at + f + 1))
                            lo(HIDL[:, f, :], T[:, f, :], HIDH[:, f, :]).then_inc(S["mlp_hid_split"], 1)
                    for f in range(KD):
                        b = 4 + f if f < 4 else f - 4
                        tile_done(ve, "mlp_down_made", f, 4, c * 4 + (n0 + 2 + f // 4), c * 6, 6 * CHUNKS * L)
                        end = v.tensor_tensor(X[:, f, :], X[:, f, :], B[b][:, :], ALU.add)
                        if last:
                            end.then_inc(S["mlp_done"], 1)
                            ve.drain().then_inc(free[b], 1)
                        else:
                            end.then_inc(free[b], 1)

                with ve.Fori(0, CHUNKS - 1) as c:
                    chunk(c, False)
                chunk(CHUNKS - 1, True)

            norm("mlp0")
            mlp(0, N_MLP0)

            norm("mix1")
            ve.wait_ge(S["tab_loaded"], 64)

            def low_qk(u, f):
                ve.wait_ge(S["dil_qk_hi"], 4 * u + f + 1)
                dh, dl = ((DQH, DQL) if f < 2 else (DKH, DKL))
                lo(in_order(dl[:, f % 2, :], u % 3), natural(B[f % 2], u % 3), in_order(dh[:, f % 2, :], u % 3))\
                    .then_inc(S["dil_qk_split"], 1)
                ve.drain().then_inc(free[f % 2], 1)

            def low_values(u):
                for j in range(2):
                    ve.wait_ge(S["dil_v_hi"], 2 * u + j + 1)
                    vj = slice(2 * j, 2 * j + 2)
                    lo(DVL[:, vj, :].rearrange("p t n -> p (t n)"), B[j][:, :],
                       DVH[:, vj, :].rearrange("p t n -> p (t n)")).then_inc(S["dil_v_split"], 1)
                    ve.drain().then_inc(free[j], 1)

            def parts(u, hh):
                t0 = 2 * (hh % 2)
                return (T[:, t0, :].rearrange("p (t n) -> p t n", t=NT),
                        T[:, t0 + 1, 0:384].rearrange("p (t n) -> p t n", t=NT - 1),
                        MXS[:, u % 3, hh, :], SUMS[:, u % 3, hh, :])

            def centre(u, hh):
                cur, prev, mx, _ = parts(u, hh)
                head, g = 4 * (u // 3) + hh, u % 3

                def logits(dst, b, m, kind):
                    v.scalar_tensor_tensor(dst, B[b][:, 0:128 * m].rearrange("p (t n) -> p t n", t=m), HEAD_DIM ** -0.5,
                                           TAB[:, kind, head, :].unsqueeze(1).to_broadcast([128, m, 128]),
                                           ALU.mult, ALU.add).then_inc(free[b], 1)

                ve.wait_ge(S["dil_s_made"], 4 * u + hh + 1)
                logits(cur, 4 + hh % 2, NT, g)
                if g == 0:
                    logits(prev, 6 + hh % 2, NT - 1, 3)
                ve.drain()
                v.reduce_max(mx, cur, AX.X)
                if g == 0:
                    v.reduce_max(ST[:, 6, 0:3], prev, AX.X)
                    ve.drain()
                    v.tensor_tensor(mx[:, 1:4], mx[:, 1:4], ST[:, 6, 0:3], ALU.max)
                ve.drain()
                v.tensor_tensor(cur, cur, mx.unsqueeze(2).to_broadcast([128, NT, 128]), ALU.subtract)
                if g == 0:
                    v.tensor_tensor(prev, prev, mx[:, 1:4].unsqueeze(2).to_broadcast([128, NT - 1, 128]), ALU.subtract)
                ve.drain().then_inc(S["dil_centred"], 1)

            def normalise(u, hh):
                cur, prev, _, sm = parts(u, hh)
                g = u % 3
                ve.wait_ge(S["dil_exp"], 4 * u + hh + 1)
                v.reduce_sum(sm, cur, AX.X)
                if g == 0:
                    v.reduce_sum(ST[:, 6, 0:3], prev, AX.X)
                    ve.drain()
                    v.tensor_tensor(sm[:, 1:4], sm[:, 1:4], ST[:, 6, 0:3], ALU.add)
                ve.drain()
                v.reciprocal(ST[:, 7, :], sm)
                ve.drain()
                v.tensor_tensor(cur, cur, ST[:, 7, :].unsqueeze(2).to_broadcast([128, NT, 128]), ALU.mult)
                if g == 0:
                    v.tensor_tensor(prev, prev, ST[:, 7, 1:4].unsqueeze(2).to_broadcast([128, NT - 1, 128]), ALU.mult)
                ve.drain().then_inc(S["dil_p_ready"], 1)

            def low_probabilities(u, hh):
                ve.wait_ge(S["dil_pt_hi"], 4 * u + hh + 1)
                lo(DPL[:, 0, :], B[4 + hh % 2][:, :], DPH[:, 0, :]).then_inc(free[4 + hh % 2], 1)
                if u % 3 == 0:
                    lo(DPL[:, 1, 0:384], B[6 + hh % 2][:, 0:384], DPH[:, 1, 0:384]).then_inc(free[6 + hh % 2], 1)
                ve.drain().then_inc(S["dil_pt_split"], 1)

            def combine(half, between):
                ve.drain().then_inc(S["dil_sums"], 1)
                ve.wait_ge(S["dil_ln"], half + 1)
                flat = [t[:, :, :, :].rearrange("p a b c -> p (a b c)") for t in (SUMS, MXS)]
                v.tensor_tensor(flat[0], flat[0], flat[1], ALU.add)
                if between is not None:
                    low_values(between)
                for pr in range(2):
                    w = 2 * half + pr
                    ve.drain()
                    for g in range(3):
                        if pr > 0 and g == 0:
                            ve.wait_ge(S["dil_lse_made"], 3 * w)
                        for e in range(2):
                            dst = LSE_COLS[g].rearrange("p (t e n) -> p e t n", t=NT, e=2)[:, e]
                            end = v.tensor_copy(dst, SUMS[:, g, 2 * pr + e, :].unsqueeze(2).to_broadcast([128, NT, 64]))
                        end.then_inc(S["dil_lse"], 1)
                    ve.wait_ge(S["dil_lse_copied"], w + 1)
                    L3, top = [LSE[:, g, :] for g in range(3)], TOP
                    v.tensor_tensor(top, L3[0], L3[1], ALU.max)
                    ve.drain()
                    v.tensor_tensor(top, top, L3[2], ALU.max)
                    ve.drain()
                    for g in range(3):
                        v.tensor_tensor(L3[g], L3[g], top, ALU.subtract)
                    ve.drain().then_inc(S["dil_lse_centred"], 1)
                    ve.wait_ge(S["dil_weights"], w + 1)
                    v.tensor_tensor(top, L3[0], L3[1], ALU.add)
                    for g in range(3):
                        v.tensor_tensor(OG[pr][:, g, :], OG[pr][:, g, :], L3[g], ALU.mult)
                    ve.drain()
                    v.tensor_tensor(top, top, L3[2], ALU.add)
                    v.tensor_tensor(OG[pr][:, 0, :], OG[pr][:, 0, :], OG[pr][:, 1, :], ALU.add)
                    ve.drain()
                    v.reciprocal(top, top)
                    v.tensor_tensor(OG[pr][:, 0, :], OG[pr][:, 0, :], OG[pr][:, 2, :], ALU.add)
                    ve.drain()
                    v.tensor_tensor(DY, OG[pr][:, 0, :], top, ALU.mult).then_inc(S["dil_y_f32"], 1)
                    ve.wait_ge(S["dil_y_hi"], w + 1)
                    lo(DYL[:, w, :], DY, DYH[:, w, :]).then_inc(S["dil_y_split"], 1)

            for f in range(4):
                low_qk(0, f)
            for u in range(6):
                more = u < 5
                if u == 3:
                    combine(0, u)
                centre(u, 0)
                centre(u, 1)
                normalise(u, 0)
                normalise(u, 1)
                if u != 3:
                    low_values(u)
                low_probabilities(u, 0)
                low_probabilities(u, 1)
                centre(u, 2)
                centre(u, 3)
                normalise(u, 2)
                if more:
                    low_qk(u + 1, 0)
                normalise(u, 3)
                low_probabilities(u, 2)
                if more:
                    low_qk(u + 1, 1)
                    low_qk(u + 1, 2)
                low_probabilities(u, 3)
                if more:
                    low_qk(u + 1, 3)
            combine(1, None)
            for f in range(KD):
                tile_done(ve, "dil_out_made", f, 4, N_DILOUT + f // 4)
                v.tensor_tensor(X[:, f, :], X[:, f, :], B[f % 4][:, :], ALU.add).then_inc(S["dil_done"], 1)
                ve.drain().then_inc(free[f % 4], 1)

            norm("mlp1")
            mlp(1, N_MLP1)

            add_squares("final", KD)
            inverse_root("final")
            for k in range(KD):
                v.scalar_tensor_tensor(ACC[:, k, :], X[:, k, :], gain("final", k), R[:, :], ALU.mult, ALU.mult)\
                    .then_inc(S["final_ready"], 1)


def _bucket(distance):
    d = np.asarray(distance)
    large = 16 + (np.log(np.maximum(d, 1).astype(np.float32) / np.float32(16)) / np.float32(np.log(2048 / 16)) * 16).astype(np.int32)
    return np.where(d < 16, d, np.minimum(large, 31))


def _constants():
    c = np.zeros((128, 3 * 128 + 8), np.float32)
    p = np.arange(128)
    c[:, 0:128] = np.eye(128)
    c[:, 128:256] = np.where(p[None, :] <= p[:, None], 0.0, NEG)
    c[:, 256:384] = p[:, None] <= p[None, :]
    c[:, 384] = (10000.0 ** (-p / 128.0)).astype(np.float32)
    c[:, 385] = (10000.0 ** (-(p % 32) / 32.0)).astype(np.float32)
    c[:, 386] = np.where((p % 64) < 32, -1.0, 1.0)
    log_g = np.log(1.0 - 2.0 ** (-5.0 - np.arange(RET_HEADS)))
    rel = np.arange(512)[None, :] - p[:, None]
    decay = np.where(rel[None] >= 0, np.exp(np.maximum(rel, 0)[None] * log_g[:, None, None]), 0.0) * RET_QK ** -0.5
    onehot = np.zeros((33, 4, 256), np.float32)
    y = np.arange(256)
    for kind, (dist, ok) in enumerate((
        (127 - y, y <= 127),
        (4 * (127 - y), y <= 127),
        (4 * (127 - y), (y <= 127) & ((127 - y) % 4 == 0)),
        (255 - y, y >= 127),
    )):
        b = np.where(ok, _bucket(np.where(ok, dist, 0)), 32)
        onehot[b, kind, y] = 1.0
    return c, decay.astype(np.float32), onehot.reshape(33, 1024)


def _blocks(w, rows, cols):
    w = w[rows][:, cols]
    return w.reshape(-1, 128, w.shape[1]).transpose(1, 0, 2).reshape(128, -1)


def _lay_out_panels(a):
    out = np.empty((NPANEL, 128, PANEL), np.float32)
    at = [0]
    every = slice(None)

    def put(*parts):
        out[at[0]] = np.concatenate(parts, axis=1)
        at[0] += 1

    def cols(start, n=256):
        return slice(start, start + n)

    w, wo = a["ret_w_in"][0], a["ret_w_out"][0]
    for h in range(RET_HEADS):
        put(_blocks(w, every, cols(256 * h)))
        put(_blocks(w, every, cols(1024 + 256 * h)))
        for j in range(2):
            put(_blocks(w, cols(512 * j, 512), cols(2048 + 512 * h, 512)))
        for j in range(2):
            put(_blocks(w, every, cols(4096 + 512 * h + 256 * j)))
        for j in range(2):
            put(_blocks(wo, cols(512 * h, 512), cols(512 * j, 512)))

    def per_layer_input(L):
        put(_blocks(a["ple_w_proj"][L], every, every))
        for j in range(4):
            put(_blocks(a["ple_w_gate"][L], every, cols(256 * j)))

    per_layer_input(0)
    w = a["mla_w_in"][0]
    for j in range(4):
        put(_blocks(w, every, cols(256 * j)))
    half = np.arange(32)
    straight = np.concatenate([half, half + 32])
    swapped = np.concatenate([half + 32, half])
    put(_blocks(w, every, 1024 + np.concatenate([straight, straight, swapped, swapped])))
    uq, uk, uv, wo = a["mla_w_uq"][0], a["mla_w_uk"][0], a["mla_w_uv"][0], a["mla_w_out"][0]
    uk, uv = uk.reshape(KV_LORA, -1), uv.reshape(KV_LORA, -1)
    for hp in range(PAIRS):
        qa, qb = 192 * 2 * hp, 192 * (2 * hp + 1)
        nope = np.concatenate([np.arange(qa, qa + 128), np.arange(qb, qb + 128)])
        rope = np.concatenate([q + 128 + o for o in (straight, swapped) for q in (qa, qb)])
        put(_blocks(uq, every, nope), _blocks(uk, every, cols(256 * hp)))
        put(_blocks(uq, every, rope), _blocks(uv, every, cols(256 * hp)))
        put(_blocks(w, every, cols(1088 + 256 * hp)))
        put(_blocks(wo, cols(256 * hp), every))
    per_layer_input(1)
    w, wo = a["a_w_in_2"][0], a["a_w_out_2"][0]
    for cc in range(2):
        for j in range(2):
            put(_blocks(w, cols(512 * j, 512), cols(1024 + 512 * cc, 512)))
    for j in range(4):
        put(_blocks(w, every, cols(256 * j)))
    for j in range(4):
        put(_blocks(wo, every, cols(256 * j)))

    def mlp(L):
        up, down = a["w_up_2"][L], a["w_down_2"][L]
        for c in range(CHUNKS):
            for j in range(2):
                put(_blocks(up, every, cols(HID * c + 256 * j)))
            for j in range(2):
                put(_blocks(down, cols(HID * c, HID), cols(512 * j, 512)))

    mlp(0)
    w, wo = a["b_w_qkv_2"][0], a["b_w_out_2"][0]
    for half_ in range(2):
        for g in range(3):
            for j in range(3):
                put(_blocks(w, every, cols(1536 * j + 512 * g + 256 * half_)))
    for j in range(2):
        put(_blocks(wo, every, cols(512 * j, 512)))
    mlp(1)
    assert at[0] == NPANEL
    return out


def _tiles(v):
    return v.reshape(-1, 128).T


def kernel(**inputs):
    import concourse.bacc as bacc
    from concourse.bass_utils import run_bass_kernel_spmd

    a = {k: np.asarray(v) for k, v in inputs.items()}
    consts, decay, onehot = _constants()
    gains = [a["pre_norm_g"][0], a["post_norm_g"][0], a["pre_norm_g"][1], a["post_norm_g"][1], a["mix_norm_g_2"][0],
             a["mlp_norm_g_2"][0], a["mix_norm_g_2"][1], a["mlp_norm_g_2"][1], a["final_norm_g_2"],
             a["mla_q_norm_g"][0], a["mla_kv_norm_g"][0], a["a_ln_g_2"][0], a["a_ln_b_2"][0]]
    arrays = {
        "panels": _lay_out_panels(a),
        "gains": np.concatenate([_tiles(g) for g in gains], axis=1),
        "xin": a["x"][0].T.reshape(KD, 128, SEQ),
        "pin": a["p"][:, 0].transpose(0, 2, 1).reshape(2, 2, 128, SEQ),
        "pos": np.broadcast_to(a["positions"].astype(np.int32), (128, SEQ)),
        "gn": a["ret_gn_g"][0].reshape(RET_HEADS, 4, 128).transpose(0, 2, 1),
        "decay": decay,
        "consts": consts,
        "rel": a["rel_bias_2"],
        "onehot": onehot,
        "wsT": a["a_w_s_2"][0].transpose(2, 0, 1),
        "bs": np.broadcast_to(a["a_b_s_2"][0], (128, GROUPS, 128)),
    }
    arrays = {k: np.ascontiguousarray(v) for k, v in arrays.items()}
    nc = bacc.Bacc("TRN2", target_bir_lowering=False, num_devices=1)
    args = {k: nc.dram_tensor(k, v.shape, mybir.dt.from_np(v.dtype), kind="ExternalInput").ap() for k, v in arrays.items()}
    out = nc.dram_tensor("out", (KD, 128, SEQ), mybir.dt.float32, kind="ExternalOutput").ap()
    scratch = nc.dram_tensor("scratch", (4, 8, 128, 256), mybir.dt.float32, kind="Internal").ap()
    xsave = nc.dram_tensor("xsave", (KD, 128, SEQ), mybir.dt.float32, kind="Internal").ap()
    program(nc, out=out, scratch=scratch, xsave=xsave, **args)
    r = run_bass_kernel_spmd(nc, [arrays], core_ids=[0])
    return r.results[0]["out"].reshape(D_MODEL, SEQ).T[None]
```
